# Optimizing a Trainium2 kernel written in Bass

```python
import jax, jax.numpy as jnp
from jax import lax
import numpy as np

D_MODEL = 2048
BATCH = 1
SEQ = 512
DEPTH = 1

GRID_W = 64
CTX_LEN = 256

MLA_HEADS = 8
MLA_NOPE = 128
MLA_ROPE = 64
MLA_QK_DIM = MLA_NOPE + MLA_ROPE
MLA_V = 128
MLA_Q_RANK = 512
MLA_KV_RANK = 256
NA_HEADS = 8
NA_HEAD_DIM = 128
NA_KH = 8
NA_KW = 16

MLA_OUT = MLA_HEADS * MLA_V
NA_WIDTH = NA_HEADS * NA_HEAD_DIM
MIX_WIDTH = MLA_OUT + NA_WIDTH
IN_MLA = MLA_Q_RANK + MLA_KV_RANK + MLA_ROPE
IN_WIDTH = IN_MLA + 3 * NA_WIDTH

N_EXPERTS = 16
EC_CAPACITY_FACTOR = 2
D_EXPERT = 1024

ROPE_THETA = 10000.0
EPS = 1e-6
Q_BLOCK = 128
N_MOD = 6
MLA_SCALE = MLA_QK_DIM ** -0.5
NA_SCALE = NA_HEAD_DIM ** -0.5

kernel_name = "hybrid_mla_natten_ec_moe_dit"

def rms_norm(x, g):
    xf = x.astype(jnp.float32)
    y = xf * lax.rsqrt(jnp.mean(xf * xf, axis=-1, keepdims=True) + EPS)
    return (y * g.astype(jnp.float32)).astype(x.dtype)

def modulate(x, shift, scale):
    return x * (1 + scale) + shift

def axial_rope_tables(n_tokens):
    t = jnp.arange(n_tokens)
    row = (t // GRID_W).astype(jnp.float32)
    col = (t % GRID_W).astype(jnp.float32)
    n_freq = MLA_ROPE // 4
    inv = ROPE_THETA ** (-jnp.arange(n_freq, dtype=jnp.float32) / n_freq)
    ang = jnp.concatenate([row[:, None] * inv, col[:, None] * inv], axis=-1)
    return jnp.cos(ang), jnp.sin(ang)

def apply_rope(x, cos, sin):
    half = MLA_ROPE // 2
    c = cos[:, None, :].astype(x.dtype)
    s = sin[:, None, :].astype(x.dtype)
    x1, x2 = x[..., :half], x[..., half:]
    return jnp.concatenate([x1 * c - x2 * s, x1 * s + x2 * c], axis=-1)

def rope_tail(t, cos, sin):
    return jnp.concatenate([t[..., :MLA_NOPE], apply_rope(t[..., MLA_NOPE:], cos, sin)], axis=-1)

def mla_q(p, g_qa, w_qb, g_q, cos, sin):
    B, T, _ = p.shape
    cq = p[..., :MLA_Q_RANK]
    q = (rms_norm(cq, g_qa) @ w_qb).reshape(B, T, MLA_HEADS, MLA_QK_DIM)
    q = rms_norm(q, g_q)
    if cos is not None:
        q = rope_tail(q, cos, sin)
    return q

def mla_kv(p, g_kva, w_kvb, g_k, cos, sin):
    B, T, _ = p.shape
    ckv = p[..., MLA_Q_RANK:MLA_Q_RANK + MLA_KV_RANK]
    k_pe = p[..., MLA_Q_RANK + MLA_KV_RANK:IN_MLA]
    kv = (rms_norm(ckv, g_kva) @ w_kvb).reshape(B, T, MLA_HEADS, MLA_NOPE + MLA_V)
    k_nope, v = kv[..., :MLA_NOPE], kv[..., MLA_NOPE:]
    k_pe = jnp.broadcast_to(k_pe[:, :, None, :], (B, T, MLA_HEADS, MLA_ROPE))
    k = rms_norm(jnp.concatenate([k_nope, k_pe], axis=-1), g_k)
    if cos is not None:
        k = rope_tail(k, cos, sin)
    return k, v

def na_q(p, g_q):
    B, T, _ = p.shape
    q = p[..., IN_MLA:IN_MLA + NA_WIDTH].reshape(B, T, NA_HEADS, NA_HEAD_DIM)
    return rms_norm(q, g_q)

def na_kv(p, g_k):
    B, T, _ = p.shape
    k = p[..., IN_MLA + NA_WIDTH:IN_MLA + 2 * NA_WIDTH].reshape(B, T, NA_HEADS, NA_HEAD_DIM)
    v = p[..., IN_MLA + 2 * NA_WIDTH:IN_WIDTH].reshape(B, T, NA_HEADS, NA_HEAD_DIM)
    return rms_norm(k, g_k), v

def context_attn(q, k, v, scale):
    s = jnp.einsum('bqhd,bkhd->bhqk', q, k, preferred_element_type=jnp.float32) * scale
    p = jax.nn.softmax(s, axis=-1).astype(v.dtype)
    return jnp.einsum('bhqk,bkhd->bqhd', p, v)

def dense_attn_with_ctx(q, k, v, k_ctx, v_ctx, scale):
    B, T, H, Dk = q.shape
    Dv = v.shape[-1]
    nb = T // Q_BLOCK
    k_all = jnp.concatenate([k, k_ctx], axis=1)
    v_all = jnp.concatenate([v, v_ctx], axis=1)
    qb = q.reshape(B, nb, Q_BLOCK, H, Dk).transpose(1, 0, 2, 3, 4)

    def block(qi):
        s = jnp.einsum('bqhd,bkhd->bhqk', qi, k_all, preferred_element_type=jnp.float32) * scale
        p = jax.nn.softmax(s, axis=-1).astype(v_all.dtype)
        return jnp.einsum('bhqk,bkhd->bqhd', p, v_all)

    o = lax.map(block, qb)
    return o.transpose(1, 0, 2, 3, 4).reshape(B, T, H, Dv)

def neighbourhood_attn_with_ctx(q, k, v, k_ctx, v_ctx, rpb, rows):
    B, T, H, D = q.shape
    kh = min(NA_KH, rows)
    kw = NA_KW
    n_loc = kh * kw
    qg = q.reshape(B, rows, GRID_W, H, D)
    kg = k.reshape(B, rows, GRID_W, H, D)
    vg = v.reshape(B, rows, GRID_W, H, D)
    col = jnp.arange(GRID_W)
    col_start = jnp.clip(col - kw // 2, 0, GRID_W - kw)
    col_idx = col_start[:, None] + jnp.arange(kw)[None, :]
    col_off = col_idx - col[:, None] + (NA_KW - 1)

    def row_block(r):
        rs = jnp.clip(r - kh // 2, 0, rows - kh)
        qr = lax.dynamic_index_in_dim(qg, r, axis=1, keepdims=False)
        kband = lax.dynamic_slice_in_dim(kg, rs, kh, axis=1)
        vband = lax.dynamic_slice_in_dim(vg, rs, kh, axis=1)
        kwin = kband[:, :, col_idx]
        vwin = vband[:, :, col_idx]
        row_off = rs + jnp.arange(kh) - r + (NA_KH - 1)
        bias = rpb[:, row_off[None, :, None], col_off[:, None, :]]
        s_loc = jnp.einsum('bqhd,brqwhd->bhqrw', qr, kwin,
                           preferred_element_type=jnp.float32) * NA_SCALE
        s_loc = s_loc + bias[None].astype(jnp.float32)
        s_ctx = jnp.einsum('bqhd,bkhd->bhqk', qr, k_ctx,
                           preferred_element_type=jnp.float32) * NA_SCALE
        s = jnp.concatenate([s_loc.reshape(B, H, GRID_W, n_loc), s_ctx], axis=-1)
        p = jax.nn.softmax(s, axis=-1).astype(v.dtype)
        p_loc = p[..., :n_loc].reshape(B, H, GRID_W, kh, kw)
        p_ctx = p[..., n_loc:]
        return (jnp.einsum('bhqrw,brqwhd->bqhd', p_loc, vwin)
                + jnp.einsum('bhqk,bkhd->bqhd', p_ctx, v_ctx))

    o = lax.map(row_block, jnp.arange(rows))
    return o.transpose(1, 0, 2, 3, 4).reshape(B, T, H, D)

def merge_heads(o_mla, o_na, g_out_mla, g_out_na, w_out):
    B, T = o_mla.shape[:2]
    a = rms_norm(o_mla.reshape(B, T, MLA_OUT), g_out_mla)
    b = rms_norm(o_na.reshape(B, T, NA_WIDTH), g_out_na)
    return jnp.concatenate([a, b], axis=-1) @ w_out

def expert_choice_ffn(h, w_router, w_gate, w_up, w_down):
    B, T, D = h.shape
    cap = EC_CAPACITY_FACTOR * T // N_EXPERTS
    aff = jax.nn.softmax(jnp.einsum('btd,de->bte', h, w_router,
                                    preferred_element_type=jnp.float32), axis=-1)
    g, idx = lax.top_k(aff.transpose(0, 2, 1), cap)
    xs = jax.vmap(lambda hb, ib: hb[ib])(h, idx)
    a = jnp.einsum('becd,edf->becf', xs, w_gate)
    u = jnp.einsum('becd,edf->becf', xs, w_up)
    y = jnp.einsum('becf,efd->becd', jax.nn.silu(a) * u, w_down) * g[..., None].astype(h.dtype)
    return jax.vmap(lambda yb, ib: jnp.zeros((T, D), yb.dtype).at[ib.reshape(-1)].add(yb.reshape(-1, D)))(y, idx)

def setup_inputs(seed: int = 0) -> dict:
    key = jax.random.key(seed)
    ks = jax.random.split(key, 32)
    f32 = jnp.float32
    D = D_MODEL

    def nrm(k, shape, scale):
        return jax.random.normal(k, shape, f32) * scale

    def gain(k, shape):
        return 1.0 + 0.02 * jax.random.normal(k, shape, f32)

    return {
        "x": nrm(ks[0], (BATCH, SEQ, D), 1.0),
        "c": nrm(ks[1], (BATCH, D), 1.0),
        "ctx": nrm(ks[2], (BATCH, CTX_LEN, D), 1.0),
        "c_ctx": nrm(ks[3], (D,), 1.0),
        "w_mod": nrm(ks[4], (DEPTH, D, N_MOD * D), 0.5 * D ** -0.5),
        "b_mod": nrm(ks[5], (DEPTH, N_MOD * D), 0.01),
        "g_norm1": gain(ks[6], (DEPTH, D)),
        "w_in": nrm(ks[7], (DEPTH, D, IN_WIDTH), D ** -0.5),
        "g_qa": gain(ks[8], (DEPTH, MLA_Q_RANK)),
        "w_qb": nrm(ks[9], (DEPTH, MLA_Q_RANK, MLA_HEADS * MLA_QK_DIM), MLA_Q_RANK ** -0.5),
        "g_kva": gain(ks[10], (DEPTH, MLA_KV_RANK)),
        "w_kvb": nrm(ks[11], (DEPTH, MLA_KV_RANK, MLA_HEADS * (MLA_NOPE + MLA_V)), MLA_KV_RANK ** -0.5),
        "g_q_mla": gain(ks[12], (DEPTH, MLA_QK_DIM)),
        "g_k_mla": gain(ks[13], (DEPTH, MLA_QK_DIM)),
        "g_q_na": gain(ks[14], (DEPTH, NA_HEAD_DIM)),
        "g_k_na": gain(ks[15], (DEPTH, NA_HEAD_DIM)),
        "rpb_na": nrm(ks[16], (DEPTH, NA_HEADS, 2 * NA_KH - 1, 2 * NA_KW - 1), 0.1),
        "g_out_mla": gain(ks[17], (DEPTH, MLA_OUT)),
        "g_out_na": gain(ks[18], (DEPTH, NA_WIDTH)),
        "w_out": nrm(ks[19], (DEPTH, MIX_WIDTH, D), MIX_WIDTH ** -0.5),
        "g_norm2": gain(ks[20], (DEPTH, D)),
        "w_router": nrm(ks[21], (DEPTH, D, N_EXPERTS), D ** -0.5),
        "w_gate": nrm(ks[22], (DEPTH, N_EXPERTS, D, D_EXPERT), D ** -0.5),
        "w_up": nrm(ks[23], (DEPTH, N_EXPERTS, D, D_EXPERT), D ** -0.5),
        "w_down": nrm(ks[24], (DEPTH, N_EXPERTS, D_EXPERT, D), D_EXPERT ** -0.5),
    }

def reference(x, c, ctx, c_ctx, w_mod, b_mod, g_norm1, w_in, g_qa, w_qb, g_kva, w_kvb,
              g_q_mla, g_k_mla, g_q_na, g_k_na, rpb_na, g_out_mla, g_out_na, w_out,
              g_norm2, w_router, w_gate, w_up, w_down):
    B, T, D = x.shape
    rows = T // GRID_W
    cos, sin = axial_rope_tables(T)
    for l in range(DEPTH):
        last = l == DEPTH - 1
        mod_lat = (jax.nn.silu(c) @ w_mod[l] + b_mod[l]).reshape(B, N_MOD, 1, D)
        mod_ctx = (jax.nn.silu(c_ctx)[None] @ w_mod[l] + b_mod[l]).reshape(1, N_MOD, 1, D)

        h = modulate(rms_norm(x, g_norm1[l]), mod_lat[:, 0], mod_lat[:, 1])
        hc = modulate(rms_norm(ctx, g_norm1[l]), mod_ctx[:, 0], mod_ctx[:, 1])
        p_lat = h @ w_in[l]
        p_ctx = hc @ w_in[l]

        q_m = mla_q(p_lat, g_qa[l], w_qb[l], g_q_mla[l], cos, sin)
        k_m, v_m = mla_kv(p_lat, g_kva[l], w_kvb[l], g_k_mla[l], cos, sin)
        kc_m, vc_m = mla_kv(p_ctx, g_kva[l], w_kvb[l], g_k_mla[l], None, None)
        o_m = dense_attn_with_ctx(q_m, k_m, v_m, kc_m, vc_m, MLA_SCALE)

        q_n = na_q(p_lat, g_q_na[l])
        k_n, v_n = na_kv(p_lat, g_k_na[l])
        kc_n, vc_n = na_kv(p_ctx, g_k_na[l])
        o_n = neighbourhood_attn_with_ctx(q_n, k_n, v_n, kc_n, vc_n, rpb_na[l], rows)

        x = x + mod_lat[:, 2] * merge_heads(o_m, o_n, g_out_mla[l], g_out_na[l], w_out[l])

        if not last:
            oc_m = context_attn(mla_q(p_ctx, g_qa[l], w_qb[l], g_q_mla[l], None, None), kc_m, vc_m, MLA_SCALE)
            oc_n = context_attn(na_q(p_ctx, g_q_na[l]), kc_n, vc_n, NA_SCALE)
            ctx = ctx + mod_ctx[:, 2] * merge_heads(oc_m, oc_n, g_out_mla[l], g_out_na[l], w_out[l])

        h2 = modulate(rms_norm(x, g_norm2[l]), mod_lat[:, 3], mod_lat[:, 4])
        x = x + mod_lat[:, 5] * expert_choice_ffn(h2, w_router[l], w_gate[l], w_up[l], w_down[l])

        if not last:
            hc2 = modulate(rms_norm(ctx, g_norm2[l]), mod_ctx[:, 3], mod_ctx[:, 4])
            ctx = ctx + mod_ctx[:, 5] * expert_choice_ffn(hc2, w_router[l], w_gate[l], w_up[l], w_down[l])
    return x


_drawn_inputs = setup_inputs


def setup_inputs(seed=0):
    import zlib

    import numpy as np

    out = dict(_drawn_inputs(seed))
    spreads = {}
    factors = {'b_mod': 3.359,
     'g_norm1': 8.0,
     'g_qa': 8.0,
     'g_kva': 8.0,
     'g_q_mla': 8.0,
     'g_k_mla': 8.0,
     'g_q_na': 8.0,
     'g_k_na': 8.0,
     'rpb_na': 8.0,
     'g_out_mla': 8.0,
     'g_out_na': 8.0,
     'g_norm2': 8.0}
    for name, (base, spread) in spreads.items():
        noise = np.random.default_rng([zlib.crc32(name.encode()), seed]).standard_normal(out[name].shape)
        drawn = base * np.exp(spread * noise) if base else spread * noise
        out[name] = __import__('jax').numpy.asarray(drawn.astype(out[name].dtype))
    for name, factor in factors.items():
        out[name] = (out[name] * factor).astype(out[name].dtype)
    return out
```

```python
from contextlib import ExitStack

import numpy as np

import concourse.bass as bass
from concourse import mybir

F32 = mybir.dt.float32
U32 = mybir.dt.uint32
ALU = mybir.AluOpType
ACT = mybir.ActivationFunctionType
AX = mybir.AxisListType

P = 128
D = 2048
KD = D // P
SEQ = 512
CTX = 256
TOK = SEQ + CTX
LT = SEQ // P
AT = TOK // P
GRID_W = 64
ROWS = SEQ // GRID_W
HEADS = 8
NOPE = 128
ROPE = 64
QK = NOPE + ROPE
VD = 128
Q_RANK = 512
KV_RANK = 256
NA_D = 128
NA_KH = 8
NA_KW = 16
IN_MLA = Q_RANK + KV_RANK + ROPE
NA_W = HEADS * NA_D
N_EXP = 16
F_EXP = 1024
CAP = 2 * SEQ // N_EXP
EPS = 1e-6
MLA_SCALE = QK ** -0.5
NA_SCALE = NA_D ** -0.5
NB = 512
MODB = D // NB
NEG = -3.0e38
OFFS = 2 * NA_KW - 1
DROWS = 2 * NA_KH - 1
BIAS_J = 2 * NA_KH - 2
BIAS_N = BIAS_J * GRID_W
UNITS = 2 * LT
PAIRS = N_EXP // 2
KF = F_EXP // P
RING = 8
PIECES = KD + KF
SLOT_AT = [5, 6, 7, 4, 2, 3, 0, 1]


def some(count):
    return not isinstance(count, int) or count > 0


def carry_wait(eng, count, passed):
    if not isinstance(count, int):
        eng.sem_inc(passed, 1)


def head_plan(prep, attend):
    plan = []
    for s in range(13):
        if attend and s == 9:
            plan.append(("combine", 0))
        if prep and s < LT + AT:
            plan.append(("mla_proj", s))
        if prep and 1 <= s <= LT + AT:
            plan.append(("mla_turn", s - 1))
        if prep and s < 2 * AT:
            plan.append(("na_half", s))
        if prep and s < LT + AT:
            plan.append(("mla_norm", s))
        if attend and s >= 5:
            plan.append(("mod", s - 5))
        if attend and 2 <= s < UNITS + 2:
            plan.append(("pv", s - 2))
        if attend and 1 <= s < UNITS + 1:
            plan.append(("turn", s - 1))
        if attend and s < UNITS:
            plan.append(("scores", s))
        if prep and s % 2 and s < 2 * AT:
            plan.append(("na_norm", s // 2))
        if prep and s % 2 == 0 and s >= 2:
            plan.append(("na_turn", s // 2 - 1))
    if attend:
        plan.append(("combine", 1))
    return plan


def place_in(plan, kinds, step):
    return [x for x in plan if x[0] in kinds].index(step)


SMALL = ("mla_proj", "mod", "combine")
TURNS = ("mla_turn", "na_turn")
PREP_SMALL = LT + AT
LOOP_SMALL = LT + AT + 8 + 2
HEAD_TURNS = LT + 2 * AT
MAXES = 3 * LT


class Arena:

    def __init__(self, tensor):
        self.tensor = tensor

    def take(self, at, *dims):
        n = int(np.prod(dims))
        flat = self.tensor[:, at:at + n]
        if len(dims) == 1:
            return flat
        names = "abc"[:len(dims)]
        sizes = dict(zip(names[1:], dims[1:]))
        return flat.rearrange(f"p ({' '.join(names)}) -> p {' '.join(names)}", **sizes)


def build_layer(nc, t, out):
    ctx = ExitStack()
    with ctx:
        def sb(name, shape, dt=F32):
            return ctx.enter_context(nc.sbuf_tensor(name, shape, dt))

        def ps(name, shape):
            return ctx.enter_context(nc.psum_tensor(name, shape, F32))

        def sem(name):
            return ctx.enter_context(nc.semaphore(name))

        def dram(name, shape):
            return nc.dram_tensor(name, shape, F32, kind="Internal").ap()

        bias_d = dram("bias_d", (HEADS, P, BIAS_N))
        modrow_d = dram("modrow_d", (4, D))
        o_d = dram("o_d", (SEQ, D))
        h2_d = dram("h2_d", (SEQ, D))

        K = 256
        arena = Arena(sb("arena", [P, 194 * K]))
        hT = arena.take(0, KD, TOK)
        slab = arena.take(48 * K, KD, 384)
        modw = [arena.take(a * K, 4, NB) for a in (72, 80, 48, 56)]
        cqT = arena.take(88 * K, Q_RANK // P, SEQ)
        ckvT = arena.take(96 * K, KV_RANK // P, TOK)
        kpe_rot = arena.take(102 * K, AT, ROPE)
        x_in = arena.take(104 * K, 2, D)
        xn = arena.take(120 * K, 2, D)
        bias_all = arena.take(136 * K, HEADS * BIAS_J, GRID_W)
        w_mla = arena.take(104 * K, KD, IN_MLA)
        raw_b = arena.take(182 * K, 2, IN_MLA)
        norm_b = arena.take(182 * K + 2 * IN_MLA, Q_RANK + KV_RANK)
        junk_b = arena.take(157 * K, IN_MLA)
        at = [104 * K]

        def head_buf(*dims):
            a = at[0]
            at[0] += int(np.prod(dims))
            return arena.take(a, *dims)

        na_qT = [head_buf(SEQ) for _ in range(2)]
        na_kT = [head_buf(TOK) for _ in range(2)]
        na_v = [head_buf(AT, NA_D) for _ in range(2)]
        m_qT = [head_buf(SEQ) for _ in range(2)]
        m_q2T = [head_buf(SEQ) for _ in range(2)]
        m_kT = [head_buf(TOK) for _ in range(2)]
        m_k2T = [head_buf(TOK) for _ in range(2)]
        m_v = [head_buf(AT, VD) for _ in range(2)]
        probs = head_buf(TOK)
        biased = head_buf(TOK)
        probsT = head_buf(AT, P)
        na_raw = head_buf(2, 256)
        na_nrm = head_buf(2, 256)
        m_raw = head_buf(2, 256)
        m_nrm = head_buf(2, QK)
        m_junk = head_buf(QK)
        na_junk = head_buf(2 * NA_D)
        o_sb = head_buf(UNITS, VD)
        wq = head_buf(Q_RANK // P, QK)
        wkv = head_buf(KV_RANK // P, NOPE + VD)
        bias_h = head_buf(BIAS_N)
        assert at[0] <= 182 * K
        w_out = [arena.take(a * K, KD, NB) for a in (0, 32)]
        o_in = arena.take(112 * K, 2, D)
        mixT = arena.take(128 * K, KD, SEQ)
        x1 = arena.take(160 * K, LT, D)
        gate1_b = arena.take(64 * K, D)
        gated = arena.take(72 * K, 2, NB)
        junk_d = arena.take(72 * K, 2, 1024)
        scale2_b = arena.take(0, D)
        shift2_b = arena.take(8 * K, D)
        h2 = arena.take(16 * K, 2, D)
        h2T = arena.take(128 * K, 2, KD, P)
        moe_w = [arena.take(16 * s * K, 4, F_EXP) for s in range(RING)]
        moe_wd = [arena.take(16 * s * K, 2, D) for s in range(RING)]
        xs = arena.take(128 * K, D)
        xsT = arena.take(136 * K, KD, P)
        gate2_b = arena.take(144 * K, D)
        act = arena.take(152 * K, F_EXP)
        actT = arena.take(156 * K, KF, P)
        y_sb = arena.take(164 * K, D)

        ident = sb("ident", [P, P])
        cos2 = sb("cos2", [P, LT, ROPE])
        sin2 = sb("sin2", [P, LT, ROPE])
        anti = arena.take(164 * K, 2 * GRID_W - 1)[0:OFFS]
        colmask = arena.take(165 * K, GRID_W)
        sel = sb("sel", [P, 2])
        rpbT = arena.take(166 * K, HEADS, DROWS)[0:OFFS]
        ccol = sb("ccol", [P, 2, KD])
        cexp = sb("cexp", [P, 2, KD])
        csil = sb("csil", [P, KD, 32])
        g1 = sb("g1", [P, KD])
        gqa = sb("gqa", [P, Q_RANK // P])
        gkva = sb("gkva", [P, KV_RANK // P])
        gq_b = sb("gq_b", [P, QK])
        gkt_b = sb("gkt_b", [P, ROPE])
        gk_nope = sb("gk_nope", [P, 1])
        gqn = sb("gqn", [P, 1])
        gkn = sb("gkn", [P, 1])
        gout = sb("gout", [P, KD])
        modcol = sb("modcol", [P, 2 * KD, 2])
        mul1 = sb("mul1", [P, KD, 2])
        halves = sb("halves", [P, 2])
        modacc = sb("modacc", [P, NB])
        brow = sb("brow", [P, NB])
        modrow = sb("modrow", [1, NB])
        w_router = arena.take(154 * K, KD, N_EXP)
        st = sb("st", [P, 64])
        rope_t = sb("rope_t", [P, 2, ROPE])
        kpe_eps = sb("kpe_eps", [P, AT])
        probs_r = sb("probs_r", [P, 2, N_EXP])
        affT = arena.take(152 * K, SEQ)
        topv = arena.take(155 * K, CAP)[0:N_EXP]
        topi = arena.take(155 * K + CAP, CAP)[0:N_EXP].bitcast(U32)
        topf = arena.take(155 * K + 2 * CAP, CAP)[0:N_EXP]
        idx_pair = sb("idx_pair", [P, PAIRS], U32)
        idx_e = sb("idx_e", [CAP, N_EXP], U32)
        g_pair = sb("g_pair", [P, PAIRS])
        idx_now = sb("idx_now", [P, 1], U32)
        idx_even = sb("idx_even", [CAP, 1], U32)
        idx_odd = sb("idx_odd", [CAP, 1], U32)
        g_now = sb("g_now", [P, 1])
        x_ss, x_ms, x_rstd = st[:, 0:2], st[:, 2:4], st[:, 4:6]
        b_ss, b_ms, b_rstd = (st[:, a:a + 6] for a in (6, 12, 18))
        m_ss, m_ms, m_rs = st[:, 24:26], st[:, 26:28], st[:, 28:30]
        n_ss, n_ms, n_rs = (st[:, a:a + 4] for a in (30, 34, 38))
        mx, nmx, lsum, rinv = st[:, 42:44], st[:, 44:45], st[:, 45:47], st[:, 47:49]
        d_ss, d_ms, d_rs = (st[:, a:a + 4] for a in (50, 54, 58))

        S = ps("S", [P, 1024])
        PT = ps("PT", [P, 1024])
        PJ = ps("PJ", [P, 512])
        MJ = ps("MJ", [P, 512])
        TR = ps("TR", [P, 512])
        O = ps("O", [P, 512])

        const_in = sem("const_in")
        zeroed = sem("zeroed")
        half_set = sem("half_set")
        c_exp, c_rec, c_sil = sem("c_exp"), sem("c_rec"), sem("c_sil")
        bt_full, bt_free, bias_out = sem("bt_full"), sem("bt_free"), sem("bias_out")
        x_got = [sem("x_got0"), sem("x_got1")]
        x_ssd, x_msd, x_rsd, x_nrm = sem("x_ssd"), sem("x_msd"), sem("x_rsd"), sem("x_nrm")
        xt_full, xt_free = sem("xt_full"), sem("xt_free")
        mod_in = [sem(f"mod_in{i}") for i in range(4)]
        brow_in = sem("brow_in")
        ma_full, ma_used, ma_sum, ma_col, ma_free = (sem(n) for n in ("ma_full", "ma_used", "ma_sum", "ma_col", "ma_free"))
        mul_set, h_ready = sem("mul_set"), sem("h_ready")
        wm_in = [sem(f"wm_in{i}") for i in range(4)]
        b_full, b_free, b_ssd, b_msd, b_rsd, b_nrm = (sem(n) for n in ("b_full", "b_free", "b_ssd", "b_msd", "b_rsd", "b_nrm"))
        bt2_full, bt2_free, kpe_g, kpe_part, kpe_done, kpe_pre = (sem(n) for n in ("bt2_full", "bt2_free", "kpe_g", "kpe_part", "kpe_done", "kpe_pre"))
        slab_in = [sem(f"slab_in{i}") for i in range(4)]
        slab_used, mw_in, bias_in = sem("slab_used"), sem("mw_in"), sem("bias_in")
        pj_full, pj_free, na_ssd, na_msd, na_rsd, na_nrmd = (sem(n) for n in ("pj_full", "pj_free", "na_ssd", "na_msd", "na_rsd", "na_nrmd"))
        mj_full, mj_free, m_ssd, m_msd, m_rsd, m_nrmd, rope_part, m_rope = (
            sem(n) for n in ("mj_full", "mj_free", "m_ssd", "m_msd", "m_rsd", "m_nrmd", "rope_part", "m_rope"))
        tr_full, tr_free = sem("tr_full"), sem("tr_free")
        s_full, mx_part, mx_done, exp_done = sem("s_full"), sem("mx_part"), sem("mx_done"), sem("exp_done")
        t_full, pt_a, pt_b, rinv_done = sem("t_full"), sem("pt_a"), sem("pt_b"), sem("rinv_done")
        v_full, o_free, o_out, modrow_out = sem("v_full"), sem("o_free"), sem("o_out"), sem("modrow_out")
        wo_in = [sem("wo_in0"), sem("wo_in1")]
        o_got = [sem("o_got0"), sem("o_got1")]
        xr_in, gate1_in = sem("xr_in"), sem("gate1_in")
        d_ssd, d_msd, d_rsd, d_nrm = sem("d_ssd"), sem("d_msd"), sem("d_rsd"), sem("d_nrm")
        dt_full, dt_free, y_full, y_free, gated_done, x1_done = (sem(n) for n in ("dt_full", "dt_free", "y_full", "y_free", "gated_done", "x1_done"))
        mod2_in, g2_in, mul2_set = sem("mod2_in"), sem("g2_in"), sem("mul2_set")
        e_ssd, e_msd, e_rsd, e_mul, h2_done = sem("e_ssd"), sem("e_msd"), sem("e_rsd"), sem("e_mul"), sem("h2_done")
        h2_out = [sem("h2_out0"), sem("h2_out1")]
        x1_out, router_in = sem("x1_out"), sem("router_in")
        et_full, et_free, lg_full, lg_mx, lg_nm, lg_exp, lg_rec, lg_aff, at_full, at_free = (
            sem(n) for n in ("et_full", "et_free", "lg_full", "lg_mx", "lg_nm", "lg_exp", "lg_rec", "lg_aff", "at_full", "at_free"))
        top_step, sp_full, idx_done = sem("top_step"), sem("sp_full"), sem("idx_done")
        moe_in = [sem(f"moe_in{i}") for i in range(RING)]
        moe_used = sem("moe_used")
        gate2_in, rows_set, pay_set, xs_in = sem("gate2_in"), sem("rows_set"), sem("pay_set"), sem("xs_in")
        xt2_full, xt2_free = sem("xt2_full"), sem("xt2_free")
        silu_done, act_done, at2_full, at2_free, y_done, sc_out = (
            sem(n) for n in ("silu_done", "act_done", "at2_full", "at2_free", "y_done", "sc_out"))

        w_in, w_mod, b_mod = t["w_in"][0], t["w_mod"][0], t["b_mod"]
        N_CONST = 19

        def mod_piece(block, kq):
            return w_mod[kq * 512:(kq + 1) * 512, bass.ts(block, NB)].rearrange("(k p) n -> p k n", p=P)

        def slab_cols(g, kq, which):
            return w_in[kq * 512:(kq + 1) * 512, bass.ds(IN_MLA + which * NA_W + g * NA_D, NA_D)].rearrange(
                "(k p) n -> p k n", p=P)

        def moe_piece(pair, i, up=0):
            if i < KD:
                w = t["w_up"][0] if up else t["w_gate"][0]
                return w[bass.ds(pair * 2, 2), i * P:(i + 1) * P, :].rearrange("e p n -> p e n")
            return t["w_down"][0][bass.ds(pair * 2, 2), (i - KD) * P:(i - KD + 1) * P, :].rearrange("e p n -> p e n")

        block = ctx.enter_context(nc.Block())

        passed = sem("passed")

        @block.sync
        def _(sp):
            for b in range(2):
                for kq in range(4):
                    if b:
                        sp.wait_ge(ma_used, 4 * (b - 1) + kq + 1)
                    sp.dma_start(modw[kq], mod_piece(b, kq)).then_inc(mod_in[kq], 16)
                if b == 0:
                    sp.wait_ge(zeroed, 2)
                else:
                    sp.wait_ge(ma_sum, b)
                sp.dma_start(brow[0:2, :], b_mod[:, b * NB:(b + 1) * NB].partition_broadcast(2)).then_inc(brow_in, 16)
            sp.wait_ge(bt_free, 16)
            sp.dma_start(bias_d.rearrange("h p n -> p h n"), bias_all.rearrange("p (h j) c -> p h (j c)", h=HEADS)).then_inc(bias_out, 16)
            with sp.Fori(2, 2 * MODB) as b:
                for kq in range(4):
                    sp.wait_ge(ma_used, 4 * (b - 1) + kq + 1)
                    sp.dma_start(modw[kq], mod_piece(b, kq)).then_inc(mod_in[kq], 16)
                sp.wait_ge(ma_sum, b)
                sp.dma_start(brow[0:2, :], b_mod[:, bass.ts(b, NB)].partition_broadcast(2)).then_inc(brow_in, 16)
            sp.wait_ge(ma_sum, 2 * MODB)
            sp.dma_start(brow[0:1, :], b_mod[:, bass.ts(2 * MODB, NB)]).then_inc(brow_in, 16)
            sp.wait_ge(xt_full, 4 * AT)
            sp.wait_ge(bias_out, 16)
            for kq in range(4):
                sp.dma_start(w_mla[:, 4 * kq:4 * kq + 4, :],
                             w_in[kq * 512:(kq + 1) * 512, 0:IN_MLA].rearrange("(k p) n -> p k n", p=P)).then_inc(wm_in[kq], 16)

            def loads(h, prep, attend, first=False):
                g = h + 1
                plan = head_plan(prep, attend)
                base = PREP_SMALL + LOOP_SMALL * h if not first else 0

                def small(step):
                    return base + place_in(plan, SMALL, step) + 1

                if prep:
                    if not first:
                        last = place_in(head_plan(True, not isinstance(h, int) or h > 0), SMALL, ("mla_proj", LT + AT - 1)) + 1
                        before = 0 if isinstance(h, int) and h == 0 else PREP_SMALL + LOOP_SMALL * (h - 1)
                        sp.wait_ge(mj_full, before + last)
                    sp.dma_start(wq[:], t["w_qb"][0][:, bass.ds(g * QK, QK)].rearrange("(k p) n -> p k n", p=P)).then_inc(mw_in, 16)
                    sp.dma_start(wkv[:], t["w_kvb"][0][:, bass.ds(g * (NOPE + VD), NOPE + VD)].rearrange("(k p) n -> p k n", p=P)).then_inc(mw_in, 16)
                    for kq in range(4):
                        if first:
                            sp.wait_ge(ma_used, 8 * MODB)
                        elif kq < 2:
                            sp.wait_ge(slab_used, h + 1)
                        else:
                            sp.wait_ge(pj_full, AT * (h + 1))
                        for which in range(3):
                            sp.dma_start(slab[:, 4 * kq:4 * kq + 4, which * NA_D:(which + 1) * NA_D],
                                         slab_cols(g, kq, which)).then_inc(slab_in[kq], 16)
                if first:
                    sp.dma_start(bias_h[:], bias_d[0]).then_inc(bias_in, 16)
                    return
                for i in range(8):
                    if i >= 2:
                        sp.wait_ge(mj_full, small(("mod", i - 2)))
                    elif isinstance(h, int) and h == 0:
                        sp.wait_ge(ma_used, 8 * MODB)
                    else:
                        sp.wait_ge(mj_full, PREP_SMALL + LOOP_SMALL * (h - 1)
                                 + place_in(head_plan(True, True), SMALL, ("mod", 6 + i)) + 1)
                    sp.dma_start(modw[i % 2], mod_piece(2 * MODB + 2 * h + i // 4, i % 4)).then_inc(mod_in[i % 2], 16)
                    if i == 4:
                        sp.wait_ge(mj_free, small(("mod", 0)))
                        sp.dma_start(brow[0:1, :], b_mod[:, bass.ts(2 * MODB + 2 * h + 1, NB)]).then_inc(brow_in, 16)
                    if i == 5 and prep:
                        sp.wait_ge(mx_done, UNITS * (h + 1))
                        sp.dma_start(bias_h[:], bias_d[bass.ds(h + 1, 1)].rearrange("a p n -> p (a n)")).then_inc(bias_in, 16)
                    if i == 7 and prep:
                        sp.wait_ge(mj_free, small(("mod", 4)))
                        sp.dma_start(brow[0:1, :], b_mod[:, bass.ts(2 * MODB + 2 * h + 2, NB)]).then_inc(brow_in, 16)

            loads(-1, True, False, first=True)
            loads(0, True, True)
            with sp.Fori(1, HEADS - 1) as h:
                loads(h, True, True)
            sp.wait_ge(pj_full, AT * HEADS)
            for nb in range(2):
                sp.dma_start(w_out[nb], t["w_out"][0][:, nb * NB:(nb + 1) * NB].rearrange("(k p) n -> p k n", p=P)).then_inc(wo_in[nb], 16)
            loads(HEADS - 1, False, True)

            sp.wait_ge(o_out, 16 * UNITS * HEADS)
            sp.wait_ge(modrow_out, 16 * 2 * HEADS)
            for i in range(LT):
                if i >= 2:
                    sp.wait_ge(dt_full, 4 * (i - 1))
                sp.dma_start(o_in[:, i % 2, :], o_d[i * P:(i + 1) * P, :]).then_inc(o_got[i % 2], 16)
                if i == 1:
                    sp.dma_start(x1[:], t["tokens"][0:SEQ, :].rearrange("(t p) n -> p t n", p=P)).then_inc(xr_in, 16)
                    sp.dma_start(gate1_b[:], modrow_d[0:1, :].partition_broadcast(P)).then_inc(gate1_in, 16)

            def moe_load(pair, i, n_slot):
                s = SLOT_AT[n_slot]
                if i < KD:
                    sp.dma_start(moe_w[s][:, 0:2, :], moe_piece(pair, i)).then_inc(moe_in[n_slot], 16)
                    sp.dma_start(moe_w[s][:, 2:4, :], moe_piece(pair, i, up=1)).then_inc(moe_in[n_slot], 16)
                else:
                    sp.dma_start(moe_wd[s], moe_piece(pair, i)).then_inc(moe_in[n_slot], 32)

            for n in range(2):
                moe_load(0, n, n)
            sp.wait_ge(dt_full, 4 * LT)
            moe_load(0, 2, 2)
            for nb in range(2, MODB):
                sp.wait_ge(y_full, LT * (nb - 1))
                sp.dma_start(w_out[nb % 2], t["w_out"][0][:, nb * NB:(nb + 1) * NB].rearrange("(k p) n -> p k n", p=P)).then_inc(wo_in[nb % 2], 16)
            sp.wait_ge(y_full, LT * 3)
            sp.dma_start(scale2_b[:], modrow_d[2:3, :].partition_broadcast(P)).then_inc(mod2_in, 16)
            sp.dma_start(shift2_b[:], modrow_d[1:2, :].partition_broadcast(P)).then_inc(mod2_in, 16)
            sp.dma_start(h2[:, 1, :], t["g_norm2"].partition_broadcast(P)).then_inc(g2_in, 16)
            sp.wait_ge(x1_done, LT * MODB)
            with nc.allow_non_contiguous_dma(reason="64-byte rows of the router"):
                sp.dma_start(w_router[:], t["w_router"][0].rearrange("(k p) e -> p k e", p=P)).then_inc(router_in, 16)
            for n in range(3, 6):
                moe_load(0, n, n)
            sp.dma_start(out[0].rearrange("(t p) n -> p t n", p=P), x1[:]).then_inc(x1_out, 16)
            for i in range(LT):
                sp.wait_ge(h2_done, i + 1)
                sp.dma_start(h2_d[i * P:(i + 1) * P, :], h2[:, i % 2, :]).then_inc(h2_out[i % 2], 16)
            sp.wait_ge(lg_full, LT)
            sp.dma_start(gate2_b[:], modrow_d[3:4, :].partition_broadcast(P)).then_inc(gate2_in, 16)
            for par in range(2):
                sp.wait_ge(h2_out[par], 16 * LT // 2)
            for n in range(6, RING):
                moe_load(0, n, n)
            with sp.Fori(0, PAIRS - 1) as pair:
                for i in range(PIECES):
                    sp.wait_ge(moe_used, PIECES * pair + i + 1)
                    carry_wait(sp, PIECES * pair + i + 1, passed)
                    n = i + RING
                    if n < PIECES:
                        moe_load(pair, n, n % RING)
                    else:
                        moe_load(pair + 1, n - PIECES, n % RING)
            for i in range(PIECES - RING):
                sp.wait_ge(moe_used, PIECES * (PAIRS - 1) + i + 1)
                moe_load(PAIRS - 1, i + RING, i % RING)
            sp.wait_ge(sc_out, 32 * PAIRS)
            sp.wait_ge(x1_out, 16)

        @block.tensor
        def _(pe):
            pe.wait_ge(const_in, 16 * N_CONST)
            for grp in range(GRID_W // 4):
                if grp >= 2:
                    pe.wait_ge(bt_free, grp - 1)
                for i in range(4):
                    c = 4 * grp + i
                    for a in range(2):
                        mm = pe.matmul(S[64 * a:64 * a + 64, 512 * (grp % 2) + i * 112:512 * (grp % 2) + (i + 1) * 112].rearrange("p (h j) -> p h j", h=HEADS),
                                       anti[:, GRID_W - 1 - c:2 * GRID_W - 1 - c], rpbT[:, :, 1 - a:1 - a + BIAS_J],
                                       start=True, stop=True)
                mm.then_inc(bt_full, 1)

            def turn_rows(tile, par, first):
                pe.wait_ge(x_nrm, tile + 1)
                for q in range(4):
                    if not (first and q < 2):
                        pe.wait_ge(xt_free, 4 * tile + q - 1)
                    bank = (TR, O)[q % 2]
                    for i in range(4):
                        k = 4 * q + i
                        mm = pe.transpose(bank[:, i * P:(i + 1) * P], xn[:, par, k * P:(k + 1) * P], ident[:])
                    mm.then_inc(xt_full, 1)

            for par in range(2):
                turn_rows(par, par, par == 0)
            with pe.Fori(1, AT // 2) as pair:
                tile = 2 * pair
                for par in range(2):
                    turn_rows(tile + par, par, False)

            pe.wait_ge(c_sil, 1)
            with pe.Fori(0, 2 * MODB) as b:
                for kq in range(4):
                    pe.wait_ge(mod_in[kq], 16 * (b + 1))
                    for j in range(4):
                        mm = pe.matmul(PJ[32 * j:32 * j + 32, :], csil[:, 4 * kq + j, :], modw[kq][:, j, :],
                                       start=(kq == 0), stop=(kq == 3))
                    mm.then_inc(ma_used, 1)
                pe.wait_ge(ma_sum, b + 1)
                for i in range(4):
                    mm = pe.matmul(MJ[:, 2 * i:2 * i + 2], modacc[:, i * P:(i + 1) * P], sel[:], start=True, stop=True)
                mm.then_inc(ma_col, 1)

            def turn_b(tile):
                pe.wait_ge(b_nrm, tile + 1)
                if some(tile):
                    pe.wait_ge(bt2_free, tile)
                if tile < LT:
                    for i in range(4):
                        pe.transpose(TR[:, i * P:(i + 1) * P], norm_b[:, i * P:(i + 1) * P], ident[:])
                for i in range(2):
                    mm = pe.transpose(O[:, i * P:(i + 1) * P], norm_b[:, Q_RANK + i * P:Q_RANK + (i + 1) * P], ident[:])
                mm.then_inc(bt2_full, 1)

            for tile in range(AT):
                bank = (S, PT)[tile % 2]
                if some(tile - 1):
                    pe.wait_ge(b_free, tile - 1)
                for k in range(KD):
                    if tile == 0:
                        pe.wait_ge(wm_in[k // 4], 16)
                        pe.wait_ge(h_ready, 2 * (k + 1))
                    lhs = hT[:, k, tile * P:(tile + 1) * P]
                    if tile < LT:
                        pe.matmul(bank[:, 0:Q_RANK], lhs, w_mla[:, k, 0:Q_RANK], start=(k == 0), stop=(k == KD - 1))
                    mm = pe.matmul(bank[:, 512:512 + IN_MLA - Q_RANK], lhs, w_mla[:, k, Q_RANK:IN_MLA],
                                   start=(k == 0), stop=(k == KD - 1))
                mm.then_inc(b_full, 1)
                if tile >= 1:
                    turn_b(tile - 1)
            turn_b(AT - 1)

            def turn_of_head(h, ap, prep, attend, first=False):
                g = h + 1
                pp = 1 - ap
                plan = head_plan(prep, attend)
                small0 = 0 if first else PREP_SMALL + LOOP_SMALL * h
                turn0 = HEAD_TURNS * g
                for step in plan:
                    kind, i = step
                    if kind in SMALL:
                        small = small0 + place_in(plan, SMALL, step)
                        if some(small):
                            pe.wait_ge(mj_free, small)
                    if kind in TURNS:
                        if some(turn0 + place_in(plan, TURNS, step)):
                            pe.wait_ge(tr_free, turn0 + place_in(plan, TURNS, step))
                    if kind == "mla_proj":
                        if i == 0:
                            pe.wait_ge(mw_in, 32 * (g + 1))
                            if first:
                                pe.wait_ge(bt2_free, AT)
                        if i < LT:
                            for k in range(Q_RANK // P):
                                mm = pe.matmul(MJ[:, 0:QK], cqT[:, k, i * P:(i + 1) * P], wq[:, k, :],
                                               start=(k == 0), stop=(k == Q_RANK // P - 1))
                        else:
                            for k in range(KV_RANK // P):
                                mm = pe.matmul(MJ[:, 0:NOPE + VD], ckvT[:, k, (i - LT) * P:(i - LT + 1) * P], wkv[:, k, :],
                                               start=(k == 0), stop=(k == KV_RANK // P - 1))
                        mm.then_inc(mj_full, 1)
                    elif kind == "mla_turn":
                        if i < LT:
                            pe.wait_ge(m_rope, LT * g + i + 1)
                        else:
                            pe.wait_ge(m_nrmd, (LT + AT) * g + i + 1)
                        pe.transpose(TR[:, 0:P], m_nrm[:, i % 2, 0:NOPE], ident[:])
                        pe.transpose(TR[0:ROPE, P:2 * P], m_nrm[:, i % 2, NOPE:QK], ident[:]).then_inc(tr_full, 1)
                    elif kind == "na_half":
                        tile, half = i // 2, i % 2
                        if half == 0:
                            if some(AT * g + tile):
                                pe.wait_ge(pj_free, AT * g + tile)
                        for k in range(8 * half, 8 * half + 8):
                            if tile == 0 and k % 4 == 0:
                                pe.wait_ge(slab_in[k // 4], 48 * (g + 1))
                            lo = 0 if tile < LT else NA_D
                            mm = pe.matmul(PJ[:, 0:3 * NA_D - lo], hT[:, k, tile * P:(tile + 1) * P], slab[:, k, lo:3 * NA_D],
                                           start=(k == 0), stop=(k == KD - 1))
                        if half:
                            mm.then_inc(pj_full, 1)
                        elif tile == AT - 1:
                            mm.then_inc(slab_used, 1)
                    elif kind == "mod":
                        pe.wait_ge(mod_in[i % 2], 16 * (2 * MODB + 4 * h + i // 2 + 1))
                        for j in range(4):
                            mm = pe.matmul(MJ[32 * j:32 * j + 32, :], csil[:, 4 * (i % 4) + j, :], modw[i % 2][:, j, :],
                                           start=True, stop=True)
                        mm.then_inc(mj_full, 1)
                    elif kind == "combine":
                        pe.matmul(MJ[0:2, :], sel[:], modacc[:], start=True, stop=True).then_inc(mj_full, 1)
                    elif kind == "scores":
                        tile = i // 2
                        if i == 0:
                            pe.wait_ge(tr_free, HEAD_TURNS * (h + 1))
                        cols = slice(tile * P, (tile + 1) * P)
                        for lo, n in ((0, SEQ), (SEQ, CTX)):
                            if i % 2 == 0:
                                pe.matmul(S[:, lo:lo + n], m_qT[ap][:, cols], m_kT[ap][:, lo:lo + n], start=True, stop=False)
                                mm = pe.matmul(S[:, lo:lo + n], m_q2T[ap][0:ROPE, cols], m_k2T[ap][0:ROPE, lo:lo + n],
                                               start=False, stop=True)
                            else:
                                mm = pe.matmul(S[:, lo:lo + n], na_qT[ap][:, cols], na_kT[ap][:, lo:lo + n], start=True, stop=True)
                        mm.then_inc(s_full, 1)
                    elif kind == "turn":
                        pe.wait_ge(exp_done, UNITS * h + i + 1)
                        for j in range(AT):
                            mm = pe.transpose(PT[:, j * P:(j + 1) * P], probs[:, j * P:(j + 1) * P], ident[:])
                        mm.then_inc(t_full, 1)
                    elif kind == "pv":
                        pe.wait_ge(pt_a, UNITS * h + i + 1)
                        pe.wait_ge(pt_b, UNITS * h + i + 1)
                        if some(UNITS * h + i):
                            pe.wait_ge(o_free, UNITS * h + i)
                        v = (m_v, na_v)[i % 2][ap]
                        for j in range(AT):
                            mm = pe.matmul(O[:, 0:VD], probsT[:, j, :], v[:, j, :], start=(j == 0), stop=(j == AT - 1))
                        mm.then_inc(v_full, 1)
                    elif kind == "na_turn":
                        pe.wait_ge(na_nrmd, AT * g + i + 1)
                        if i < LT:
                            pe.transpose(TR[:, 0:P], na_nrm[:, i % 2, 0:P], ident[:])
                        pe.transpose(TR[:, P:2 * P], na_nrm[:, i % 2, P:2 * P], ident[:]).then_inc(tr_full, 1)

            turn_of_head(-1, 1, True, False, first=True)
            turn_of_head(0, 0, True, True)
            with pe.Fori(0, (HEADS - 2) // 2) as two:
                turn_of_head(2 * two + 1, 1, True, True)
                turn_of_head(2 * two + 2, 0, True, True)
            turn_of_head(HEADS - 1, 1, False, True)

            for tile in range(LT):
                pe.wait_ge(d_nrm, tile + 1)
                for q in range(4):
                    n = 4 * tile + q
                    if some(n - 1):
                        pe.wait_ge(dt_free, n - 1)
                    bank = (TR, PT)[n % 2]
                    for i in range(4):
                        k = 4 * q + i
                        mm = pe.transpose(bank[:, i * P:(i + 1) * P], o_in[:, tile % 2, k * P:(k + 1) * P], ident[:])
                    mm.then_inc(dt_full, 1)
            pe.wait_ge(dt_free, 4 * LT)
            with pe.Fori(0, MODB // 2) as two:
                for half in range(2):
                    pe.wait_ge(wo_in[half], 16 * two + 16)
                    for tile in range(LT):
                        pe.wait_ge(y_free, LT * (2 * two + half) + tile + 1)
                        bank = (PJ, MJ)[tile % 2]
                        for k in range(KD):
                            mm = pe.matmul(bank[:], mixT[:, k, tile * P:(tile + 1) * P], w_out[half][:, k, :],
                                           start=(k == 0), stop=(k == KD - 1))
                        mm.then_inc(y_full, 1)

            def router(tile):
                pe.wait_ge(et_free, 4 * (tile + 1))
                if some(tile):
                    pe.wait_ge(at_free, tile)
                pe.wait_ge(router_in, 16)
                for k in range(KD):
                    mm = pe.matmul(O[:, 0:N_EXP], h2T[:, tile % 2, k, :], w_router[:, k, :], start=(k == 0), stop=(k == KD - 1))
                mm.then_inc(lg_full, 1)

            def turn_aff(tile):
                pe.wait_ge(lg_aff, tile + 1)
                pe.transpose(O[0:N_EXP, P:2 * P], probs_r[:, tile % 2, :], ident[:]).then_inc(at_full, 1)

            for tile in range(LT):
                pe.wait_ge(h2_done, tile + 1)
                for q in range(4):
                    n = 4 * tile + q
                    if some(n - 1):
                        pe.wait_ge(et_free, n - 1)
                    bank = (TR, PT)[n % 2]
                    for i in range(4):
                        k = 4 * q + i
                        mm = pe.transpose(bank[:, i * P:(i + 1) * P], h2[:, tile % 2, k * P:(k + 1) * P], ident[:])
                    mm.then_inc(et_full, 1)
                if tile >= 1:
                    turn_aff(tile - 1)
                router(tile)
            turn_aff(LT - 1)
            pe.wait_ge(top_step, 3 * CAP // 8 + 1)
            for src, lo in ((topf, 0), (topv, 32)):
                for half in range(2):
                    mm = pe.matmul(O[64 * half:64 * half + CAP, lo:lo + N_EXP], src[:], ident[0:N_EXP, 0:N_EXP],
                                   start=True, stop=True)
            mm.then_inc(sp_full, 1)

            def turn_xs(pair):
                pe.wait_ge(xs_in, 16 * (pair + 1))
                for q in range(4):
                    if some(4 * pair + q - 1):
                        pe.wait_ge(xt2_free, 4 * pair + q - 1)
                    bank = (TR, O)[q % 2]
                    for i in range(4):
                        k = 4 * q + i
                        mm = pe.transpose(bank[:, i * P:(i + 1) * P], xs[:, k * P:(k + 1) * P], ident[:])
                    mm.then_inc(xt2_full, 1)

            GU = [S[:, 0:512], S[:, 512:1024], PT[:, 0:512], PT[:, 512:1024]]

            def expert_pair(pair, last):
                pe.wait_ge(xt2_free, 4 * (pair + 1))
                if some(4 * pair):
                    pe.wait_ge(y_done, 4 * pair)
                for k in range(KD):
                    pe.wait_ge(moe_in[k % RING], 32 * (3 * pair + k // RING + 1))
                    w = moe_w[SLOT_AT[k % RING]]
                    for b in range(4):
                        for e in range(2):
                            mm = pe.matmul(GU[b][64 * e:64 * e + CAP, :], xsT[:, k, 64 * e:64 * e + CAP],
                                           w[:, 2 * (b // 2) + e, (b % 2) * NB:(b % 2 + 1) * NB],
                                           start=(k == 0), stop=(k == KD - 1))
                    mm.then_inc(moe_used, 1)
                if not last:
                    turn_xs(pair + 1)
                pe.wait_ge(act_done, 2 * (pair + 1))
                for q in range(2):
                    if some(2 * pair + q):
                        pe.wait_ge(at2_free, 2 * pair + q)
                    for i in range(4):
                        f = 4 * q + i
                        mm = pe.transpose(PJ[:, i * P:(i + 1) * P] if q == 0 else MJ[:, i * P:(i + 1) * P],
                                          act[:, f * P:(f + 1) * P], ident[:])
                    mm.then_inc(at2_full, 1)
                pe.wait_ge(at2_free, 2 * pair + 2)
                for f in range(KF):
                    n = KD + f
                    pe.wait_ge(moe_in[n % RING], 32 * (3 * pair + n // RING + 1))
                    w = moe_wd[SLOT_AT[n % RING]]
                    for b in range(4):
                        for e in range(2):
                            mm = pe.matmul(GU[b][64 * e:64 * e + CAP, :], actT[:, f, 64 * e:64 * e + CAP],
                                           w[:, e, b * NB:(b + 1) * NB], start=(f == 0), stop=(f == KF - 1))
                    mm.then_inc(moe_used, 1)

            turn_xs(0)
            expert_pair(0, False)
            with pe.Fori(1, PAIRS - 1) as pair:
                expert_pair(pair, False)
            expert_pair(PAIRS - 1, True)

        @block.scalar
        def _(sc):
            sc.dma_start(ident[:], t["ident"]).then_inc(const_in, 16)
            sc.dma_start(anti[:], t["anti"]).then_inc(const_in, 16)
            sc.dma_start(colmask[:], t["colmask"]).then_inc(const_in, 16)
            with nc.allow_non_contiguous_dma(reason="small vectors onto the partitions"):
                sc.dma_start(rpbT[:], t["rpb_na"][0].rearrange("h r o -> o h r")).then_inc(const_in, 16)
                sc.dma_start(ccol[:, 0, :], t["c"].rearrange("b (k p) -> p (b k)", p=P)).then_inc(const_in, 16)
                sc.dma_start(ccol[:, 1, :], t["c_ctx"].rearrange("(k p) -> p k", p=P)).then_inc(const_in, 16)
                for dst, name in ((g1, "g_norm1"), (gqa, "g_qa"), (gkva, "g_kva"), (gqn, "g_q_na"), (gkn, "g_k_na")):
                    sc.dma_start(dst[:], t[name].rearrange("l (k p) -> p (l k)", p=P)).then_inc(const_in, 16)
                sc.dma_start(gk_nope[:], t["g_k_mla"][:, 0:NOPE].rearrange("l (k p) -> p (l k)", p=P)).then_inc(const_in, 16)
                sc.dma_start(gout[:, 0:8], t["g_out_mla"].rearrange("l (k p) -> p (l k)", p=P)).then_inc(const_in, 16)
                sc.dma_start(gout[:, 8:16], t["g_out_na"].rearrange("l (k p) -> p (l k)", p=P)).then_inc(const_in, 16)
            sc.dma_start(gq_b[:], t["g_q_mla"].partition_broadcast(P)).then_inc(const_in, 16)
            sc.dma_start(gkt_b[:], t["g_k_mla"][:, NOPE:QK].partition_broadcast(P)).then_inc(const_in, 16)
            sc.dma_start(cos2[:], t["cos2"]).then_inc(const_in, 16)
            sc.dma_start(sin2[:], t["sin2"]).then_inc(const_in, 16)
            sc.dma_start(sel[:], t["sel"]).then_inc(const_in, 16)
            sc.wait_ge(const_in, 16 * N_CONST)
            sc.activation(cexp[:], ccol[:], ACT.Exp, scale=-1.0).then_inc(c_exp, 1)

            def norm_rows(tile, par, n_par):
                sc.wait_ge(x_got[par], 16 * (n_par + 1))
                if some(4 * (tile - 1)):
                    sc.wait_ge(xt_full, 4 * (tile - 1))
                sc.activation(xn[:, par, :], x_in[:, par, :], ACT.Square, accum_out=x_ss[:, par:par + 1]).then_inc(x_ssd, 1)
                sc.wait_ge(x_rsd, tile + 1)
                sc.wait_ge(x_ssd, tile + 1)
                sc.activation(xn[:, par, :], x_in[:, par, :], ACT.Copy, scale=x_rstd[:, par:par + 1]).then_inc(x_nrm, 1)

            for par in range(2):
                norm_rows(par, par, 0)
            with sc.Fori(1, AT // 2) as pair:
                for par in range(2):
                    norm_rows(2 * pair + par, par, pair)

            for tile in range(AT):
                sc.wait_ge(b_free, tile + 1)
                r = raw_b[:, tile % 2, :]
                if tile < LT:
                    sc.activation(junk_b[:, 0:Q_RANK], r[:, 0:Q_RANK], ACT.Square,
                                  accum_out=b_ss[:, tile % 2 * 3:tile % 2 * 3 + 1])
                sc.activation(junk_b[:, Q_RANK:Q_RANK + KV_RANK], r[:, Q_RANK:Q_RANK + KV_RANK], ACT.Square,
                              accum_out=b_ss[:, tile % 2 * 3 + 1:tile % 2 * 3 + 2])
                sc.activation(junk_b[:, Q_RANK + KV_RANK:IN_MLA], r[:, Q_RANK + KV_RANK:IN_MLA], ACT.Square,
                              accum_out=b_ss[:, tile % 2 * 3 + 2:tile % 2 * 3 + 3]).then_inc(b_ssd, 1)

            def turn_of_head(h, prep, attend, first=False):
                g = h + 1
                plan = head_plan(prep, attend)
                small0 = 0 if first else PREP_SMALL + LOOP_SMALL * h
                for step in plan:
                    kind, i = step
                    if kind == "mla_proj":
                        sc.wait_ge(mj_free, small0 + place_in(plan, SMALL, step) + 1)
                        if some((LT + AT) * g + i):
                            sc.wait_ge(m_ssd, (LT + AT) * g + i)
                        n = QK if i < LT else NOPE
                        sc.activation(m_junk[:, 0:n], m_raw[:, i % 2, 0:n], ACT.Square,
                                      accum_out=m_ss[:, i % 2:i % 2 + 1]).then_inc(m_ssd, 1)
                    elif kind == "na_half" and i % 2:
                        tile = i // 2
                        sc.wait_ge(pj_free, AT * g + tile + 1)
                        if some(AT * g + tile):
                            sc.wait_ge(na_ssd, AT * g + tile)
                        if tile < LT:
                            sc.activation(na_junk[:, 0:P], na_raw[:, tile % 2, 0:P], ACT.Square,
                                          accum_out=n_ss[:, 2 * (tile % 2):2 * (tile % 2) + 1])
                        sc.activation(na_junk[:, P:2 * P], na_raw[:, tile % 2, P:2 * P], ACT.Square,
                                      accum_out=n_ss[:, 2 * (tile % 2) + 1:2 * (tile % 2) + 2]).then_inc(na_ssd, 1)
                    elif kind == "scores":
                        sc.wait_ge(mx_done, UNITS * h + i + 1)
                        src = S[:, 0:TOK] if i % 2 == 0 else biased
                        sc.activation(probs[:], src, ACT.Exp, bias=nmx, accum_out=lsum[:, i % 2:i % 2 + 1]).then_inc(exp_done, 1)
                    elif kind == "turn":
                        sc.wait_ge(t_full, UNITS * h + i + 1)
                        sc.copy(probsT[:, 4:6, :], PT[:, 512:768].rearrange("p (a b) -> p a b", b=P)).then_inc(pt_b, 1)
                    elif kind == "pv":
                        sc.wait_ge(v_full, UNITS * h + i + 1)
                        sc.wait_ge(rinv_done, UNITS * h + i + 1)
                        if i == 0:
                            if some(16 * UNITS * h):
                                sc.wait_ge(o_out, 16 * UNITS * h)
                        sc.activation(o_sb[:, i, :], O[:, 0:VD], ACT.Copy, scale=rinv[:, i % 2:i % 2 + 1]).then_inc(o_free, 1)
                        sc.wait_ge(o_free, UNITS * h + i + 1)
                        tile, group = i // 2, i % 2
                        sc.dma_start(o_d[tile * P:(tile + 1) * P, bass.ds(group * HEADS * VD + h * VD, VD)],
                                     o_sb[:, i, :]).then_inc(o_out, 16)
                    elif kind == "combine":
                        sc.wait_ge(mj_free, small0 + place_in(plan, SMALL, step) + 1)
                        sc.dma_start(modrow_d.rearrange("a (b n) -> (a b) n", n=NB)[bass.ds(2 * h + i, 1), :],
                                     modrow[:]).then_inc(modrow_out, 16)

            turn_of_head(-1, True, False, first=True)
            turn_of_head(0, True, True)
            with sc.Fori(1, HEADS - 1) as h:
                turn_of_head(h, True, True)
            turn_of_head(HEADS - 1, False, True)

            for tile in range(LT):
                sc.wait_ge(o_got[tile % 2], 16 * (tile // 2 + 1))
                for half in range(2):
                    rows = o_in[:, tile % 2, half * 1024:(half + 1) * 1024]
                    last = sc.activation(junk_d[:, half, :], rows, ACT.Square, accum_out=d_ss[:, 2 * (tile % 2) + half:2 * (tile % 2) + half + 1])
                last.then_inc(d_ssd, 1)
                sc.wait_ge(d_rsd, tile + 1)
                sc.wait_ge(d_ssd, tile + 1)
                for half in range(2):
                    rows = o_in[:, tile % 2, half * 1024:(half + 1) * 1024]
                    last = sc.activation(rows, rows, ACT.Copy, scale=d_rs[:, 2 * (tile % 2) + half:2 * (tile % 2) + half + 1])
                last.then_inc(d_nrm, 1)

            def router_exp(tile):
                sc.wait_ge(lg_nm, tile + 1)
                sc.activation(probs_r[:, tile % 2, :], O[:, 0:N_EXP], ACT.Exp, bias=nmx,
                              accum_out=lsum[:, tile % 2:tile % 2 + 1]).then_inc(lg_exp, 1)

            def square(tile):
                sc.wait_ge(x1_done, LT * (MODB - 1) + tile + 1)
                if tile == 1:
                    sc.wait_ge(mul2_set, 1)
                if tile >= 2:
                    sc.wait_ge(h2_out[tile % 2], 16)
                    sc.wait_ge(et_full, 4 * (tile - 1))
                sc.activation(h2[:, tile % 2, :], x1[:, tile, :], ACT.Square, accum_out=d_ss[:, tile:tile + 1]).then_inc(e_ssd, 1)

            square(0)
            square(1)
            for tile in range(LT):
                router_exp(tile)
                if tile + 2 < LT:
                    square(tile + 2)

            def expert_pair(pair):
                sc.wait_ge(moe_used, PIECES * pair + KD)
                if some(2 * pair):
                    sc.wait_ge(at2_full, 2 * pair)
                for b in range(2):
                    sc.activation(act[:, b * NB:(b + 1) * NB], S[:, b * NB:(b + 1) * NB], ACT.Silu).then_inc(silu_done, 1)

            expert_pair(0)
            with sc.Fori(1, PAIRS) as pair:
                expert_pair(pair)

        @block.gpsimd
        def _(po):
            po.memset(csil[:], 0.0).then_inc(zeroed, 1)
            po.memset(brow[:], 0.0).then_inc(zeroed, 1)
            po.memset(halves[:], -0.5).then_inc(half_set, 1)
            for par in range(2):
                po.dma_start(x_in[:, par, :], t["tokens"][par * P:(par + 1) * P, :]).then_inc(x_got[par], 16)
            po.wait_ge(half_set, 1)

            def root(ms, out_ap, done, n=1):
                po.tensor_tensor(out_ap, ms, halves[:, 0:n], ALU.pow).then_inc(done, 1)

            def row_rstd(tile, par):
                po.wait_ge(x_ssd, tile + 1)
                carry_wait(po, tile + 1, passed)
                po.tensor_scalar(x_ms[:, par:par + 1], x_ss[:, par:par + 1], 1.0 / D, EPS, ALU.mult, ALU.add).then_inc(x_msd, 1)
                po.wait_ge(x_msd, tile + 1)
                root(x_ms[:, par:par + 1], x_rstd[:, par:par + 1], x_rsd)

            for par in range(2):
                row_rstd(par, par)
            with po.Fori(1, AT // 2) as pair:
                tile = 2 * pair
                for par in range(2):
                    po.wait_ge(x_nrm, tile + par - 1)
                    carry_wait(po, tile + par - 1, passed)
                    po.dma_start(x_in[:, par, :], t["tokens"][bass.ds((tile + par) * P, P), :]).then_inc(x_got[par], 16)
                for par in range(2):
                    row_rstd(tile + par, par)

            def rotate(dst, rows, tile, scratch, done, n0):
                half = ROPE // 2
                po.tensor_tensor(scratch[:, 0, :], rows, cos2[:, tile, :], ALU.mult).then_inc(done, 1)
                po.tensor_tensor(scratch[:, 1, 0:half], rows[:, half:ROPE], sin2[:, tile, 0:half], ALU.mult).then_inc(done, 1)
                po.tensor_tensor(scratch[:, 1, half:ROPE], rows[:, 0:half], sin2[:, tile, half:ROPE], ALU.mult).then_inc(done, 1)
                po.wait_ge(done, n0 + 3)
                return po.tensor_tensor(dst, scratch[:, 0, :], scratch[:, 1, :], ALU.add)

            for tile in range(AT):
                p3 = tile % 2 * 3
                po.wait_ge(b_ssd, tile + 1)
                if tile < LT:
                    po.tensor_scalar(b_ms[:, p3:p3 + 1], b_ss[:, p3:p3 + 1], 1.0 / Q_RANK, EPS, ALU.mult, ALU.add)
                po.tensor_scalar(kpe_eps[:, tile:tile + 1], b_ss[:, p3 + 2:p3 + 3], 1.0 / QK, EPS, ALU.mult, ALU.add).then_inc(kpe_pre, 1)
                po.tensor_scalar(b_ms[:, p3 + 1:p3 + 2], b_ss[:, p3 + 1:p3 + 2], 1.0 / KV_RANK, EPS, ALU.mult, ALU.add).then_inc(b_msd, 1)
                po.wait_ge(b_msd, tile + 1)
                if tile < LT:
                    root(b_ms[:, p3:p3 + 2], b_rstd[:, p3:p3 + 2], b_rsd, 2)
                else:
                    root(b_ms[:, p3 + 1:p3 + 2], b_rstd[:, p3 + 1:p3 + 2], b_rsd)
                if tile < LT:
                    po.wait_ge(kpe_g, tile + 1)
                    rotate(kpe_rot[:, tile, :], kpe_rot[:, tile, :], tile, rope_t, kpe_part, 3 * tile).then_inc(kpe_done, 1)
                    po.wait_ge(kpe_done, tile + 1)

            def turn_of_head(h, prep, attend):
                g = h + 1
                for kind, i in head_plan(prep, attend):
                    if kind == "mla_proj":
                        n = (LT + AT) * g + i + 1
                        one = slice(i % 2, i % 2 + 1)
                        po.wait_ge(m_ssd, n)
                        carry_wait(po, n, passed)
                        if i < LT:
                            po.tensor_scalar(m_ms[:, one], m_ss[:, one], 1.0 / QK, EPS, ALU.mult, ALU.add).then_inc(m_msd, 1)
                        else:
                            po.tensor_scalar(m_ms[:, one], m_ss[:, one], 1.0 / QK, kpe_eps[:, i - LT:i - LT + 1],
                                             ALU.mult, ALU.add).then_inc(m_msd, 1)
                        po.wait_ge(m_msd, n)
                        root(m_ms[:, one], m_rs[:, one], m_rsd)
                    elif kind == "mla_norm" and i < LT:
                        po.wait_ge(m_nrmd, (LT + AT) * g + i + 1)
                        carry_wait(po, (LT + AT) * g + i + 1, passed)
                        tail = m_nrm[:, i % 2, NOPE:QK]
                        rotate(tail, tail, i, rope_t, rope_part, 3 * (LT * g + i)).then_inc(m_rope, 1)
                        po.wait_ge(m_rope, LT * g + i + 1)
                        carry_wait(po, LT * g + i + 1, passed)
                    elif kind == "na_half" and i % 2:
                        tile = i // 2
                        two = slice(2 * (tile % 2), 2 * (tile % 2) + 2) if tile < LT else slice(2 * (tile % 2) + 1, 2 * (tile % 2) + 2)
                        po.wait_ge(na_ssd, AT * g + tile + 1)
                        carry_wait(po, AT * g + tile + 1, passed)
                        po.tensor_scalar(n_ms[:, two], n_ss[:, two], 1.0 / NA_D, EPS, ALU.mult, ALU.add).then_inc(na_msd, 1)
                        po.wait_ge(na_msd, AT * g + tile + 1)
                        root(n_ms[:, two], n_rs[:, two], na_rsd, 2 if tile < LT else 1)

            turn_of_head(-1, True, False)
            turn_of_head(0, True, True)
            with po.Fori(1, HEADS - 1) as h:
                turn_of_head(h, True, True)

            for tile in range(LT):
                two = slice(2 * (tile % 2), 2 * (tile % 2) + 2)
                po.wait_ge(d_ssd, tile + 1)
                po.tensor_scalar(d_ms[:, two], d_ss[:, two], 1.0 / (HEADS * VD), EPS, ALU.mult, ALU.add).then_inc(d_msd, 1)
                po.wait_ge(d_msd, tile + 1)
                root(d_ms[:, two], d_rs[:, two], d_rsd, 2)
            for tile in range(LT):
                one = slice(tile, tile + 1)
                po.wait_ge(e_ssd, tile + 1)
                po.tensor_scalar(d_ms[:, one], d_ss[:, one], 1.0 / D, EPS, ALU.mult, ALU.add).then_inc(e_msd, 1)
                po.wait_ge(e_msd, tile + 1)
                root(d_ms[:, one], d_rs[:, one], e_rsd)

            def gather(pair):
                po.wait_ge(rows_set, pair + 1)
                carry_wait(po, pair + 1, passed)
                po.indirect_dma_start(xs[:], None, h2_d, bass.IndirectOffsetOnAxis(ap=idx_now[:, 0:1], axis=0)).then_inc(xs_in, 16)

            def scatter(pair):
                po.wait_ge(pay_set, 3 * (pair + 1))
                carry_wait(po, 3 * (pair + 1), passed)
                po.wait_ge(y_done, 4 * (pair + 1))
                carry_wait(po, 4 * (pair + 1), passed)
                po.indirect_dma_start(out[0], bass.IndirectOffsetOnAxis(ap=idx_even[:, 0:1], axis=0), y_sb[0:CAP, :], None,
                                      compute_op=ALU.add).then_inc(sc_out, 16)
                po.wait_ge(sc_out, 32 * pair + 16)
                carry_wait(po, 32 * pair + 16, passed)
                po.indirect_dma_start(out[0], bass.IndirectOffsetOnAxis(ap=idx_odd[:, 0:1], axis=0), y_sb[64:64 + CAP, :], None,
                                      compute_op=ALU.add).then_inc(sc_out, 16)
                po.wait_ge(sc_out, 32 * pair + 32)
                carry_wait(po, 32 * pair + 32, passed)

            for par in range(2):
                po.wait_ge(h2_out[par], 16 * LT // 2)
            po.wait_ge(x1_out, 16)
            gather(0)

            def expert_pair(pair, last):
                if not last:
                    po.wait_ge(xt2_full, 4 * (pair + 1))
                    carry_wait(po, 4 * (pair + 1), passed)
                    gather(pair + 1)
                scatter(pair)

            expert_pair(0, False)
            with po.Fori(1, PAIRS - 1) as pair:
                expert_pair(pair, False)
            expert_pair(PAIRS - 1, True)

        @block.vector
        def _(ve):
            ve.wait_ge(const_in, 16 * N_CONST)
            for grp in range(GRID_W // 4):
                ve.wait_ge(bt_full, grp + 1)
                cols = slice(4 * grp, 4 * grp + 4)
                ve.tensor_tensor(bias_all[:, :, cols].rearrange("p r c -> p c r"),
                                 S[:, 512 * (grp % 2):512 * (grp % 2) + 448].rearrange("p (c r) -> p c r", c=4),
                                 colmask[:, cols].unsqueeze(2).broadcast_to([P, 4, HEADS * BIAS_J]), ALU.add).then_inc(bt_free, 1)
            ve.wait_ge(c_exp, 1)
            ve.tensor_scalar(cexp[:], cexp[:], 1.0, None, ALU.add).then_inc(c_rec, 1)
            ve.wait_ge(c_rec, 1)
            ve.reciprocal(cexp[:], cexp[:]).then_inc(c_rec, 1)
            ve.wait_ge(c_rec, 2)
            ve.wait_ge(zeroed, 2)
            ve.tensor_tensor(csil[:, :, 0:2].rearrange("p k c -> p c k"), ccol[:], cexp[:], ALU.mult).then_inc(c_sil, 1)

            def copy_turned(tile):
                for q in range(4):
                    ve.wait_ge(xt_full, 4 * tile + q + 1)
                    bank = (TR, O)[q % 2]
                    ve.tensor_copy(hT[:, 4 * q:4 * q + 4, bass.ds(tile * P, P)],
                                   bank[:].rearrange("p (a b) -> p a b", b=P)).then_inc(xt_free, 1)

            with ve.Fori(0, AT) as tile:
                copy_turned(tile)
            with ve.Fori(0, 2 * MODB) as b:
                ve.wait_ge(ma_used, 4 * b + 4)
                ve.wait_ge(brow_in, 16 * (b + 1))
                ve.tensor_tensor(modacc[:], PJ[:], brow[:], ALU.add).then_inc(ma_sum, 1)
                ve.wait_ge(ma_col, b + 1)
                ve.tensor_copy(modcol[:, bass.ds(4 * b, 4), :], MJ[:, 0:8].rearrange("p (a b) -> p a b", b=2)).then_inc(ma_free, 1)
            ve.wait_ge(ma_free, 2 * MODB)
            ve.scalar_tensor_tensor(mul1[:], modcol[:, KD:2 * KD, :], 1.0, g1[:].unsqueeze(2).broadcast_to([P, KD, 2]),
                                    ALU.add, ALU.mult).then_inc(mul_set, 1)
            ve.wait_ge(mul_set, 1)
            ve.wait_ge(xt_free, 4 * AT)
            for k in range(KD):
                for c, (lo, hi) in enumerate(((0, SEQ), (SEQ, TOK))):
                    ve.tensor_scalar(hT[:, k, lo:hi], hT[:, k, lo:hi], mul1[:, k, c:c + 1], modcol[:, k, c:c + 1],
                                     ALU.mult, ALU.add).then_inc(h_ready, 1)

            def copy_b(tile):
                ve.wait_ge(bt2_full, tile + 1)
                cols = slice(tile * P, (tile + 1) * P)
                if tile < LT:
                    for i in range(4):
                        ve.tensor_scalar(cqT[:, i, cols], TR[:, i * P:(i + 1) * P], gqa[:, i:i + 1], None, ALU.mult)
                for i in range(2):
                    last = ve.tensor_scalar(ckvT[:, i, cols], O[:, i * P:(i + 1) * P], gkva[:, i:i + 1], None, ALU.mult)
                last.then_inc(bt2_free, 1)

            for tile in range(AT):
                ve.wait_ge(b_full, tile + 1)
                bank = (S, PT)[tile % 2]
                r = raw_b[:, tile % 2, :]
                if tile < LT:
                    ve.tensor_copy(r[:, 0:Q_RANK], bank[:, 0:Q_RANK])
                ve.tensor_copy(r[:, Q_RANK:IN_MLA], bank[:, 512:512 + IN_MLA - Q_RANK]).then_inc(b_free, 1)
                if tile >= 1:
                    copy_b(tile - 1)
                ve.wait_ge(b_free, tile + 1)
                ve.tensor_tensor(kpe_rot[:, tile, :], r[:, Q_RANK + KV_RANK:IN_MLA], gkt_b[:], ALU.mult).then_inc(kpe_g, 1)
                ve.wait_ge(b_rsd, tile + 1)
                p3 = tile % 2 * 3
                if tile < LT:
                    ve.tensor_scalar(norm_b[:, 0:Q_RANK], r[:, 0:Q_RANK], b_rstd[:, p3:p3 + 1], None, ALU.mult)
                ve.tensor_scalar(norm_b[:, Q_RANK:Q_RANK + KV_RANK], r[:, Q_RANK:Q_RANK + KV_RANK], b_rstd[:, p3 + 1:p3 + 2],
                                 None, ALU.mult).then_inc(b_nrm, 1)
            copy_b(AT - 1)
            ve.tensor_scalar(gq_b[:], gq_b[:], MLA_SCALE, None, ALU.mult).then_inc(mul_set, 1)
            ve.tensor_scalar(gqn[:], gqn[:], NA_SCALE, None, ALU.mult).then_inc(mul_set, 1)
            ve.wait_ge(mul_set, 3)
            ve.wait_ge(kpe_done, LT)

            def turn_of_head(h, ap, prep, attend, first=False):
                g = h + 1
                pp = 1 - ap
                plan = head_plan(prep, attend)
                small0 = 0 if first else PREP_SMALL + LOOP_SMALL * h
                turn0 = HEAD_TURNS * g
                for step in plan:
                    kind, i = step
                    if kind in SMALL:
                        small = small0 + place_in(plan, SMALL, step)
                        ve.wait_ge(mj_full, small + 1)
                    if kind in TURNS:
                        ve.wait_ge(tr_full, turn0 + place_in(plan, TURNS, step) + 1)
                    if kind == "mla_proj":
                        if i < LT:
                            ve.tensor_copy(m_raw[:, i % 2, 0:QK], MJ[:, 0:QK]).then_inc(mj_free, 1)
                        else:
                            ve.tensor_copy(m_v[pp][:, i - LT, :], MJ[:, NOPE:NOPE + VD])
                            ve.tensor_copy(m_raw[:, i % 2, 0:NOPE], MJ[:, 0:NOPE]).then_inc(mj_free, 1)
                    elif kind == "mla_norm":
                        ve.wait_ge(m_rsd, (LT + AT) * g + i + 1)
                        one = m_rs[:, i % 2:i % 2 + 1]
                        if i < LT:
                            ve.scalar_tensor_tensor(m_nrm[:, i % 2, :], m_raw[:, i % 2, 0:QK], one, gq_b[:],
                                                    ALU.mult, ALU.mult).then_inc(m_nrmd, 1)
                        else:
                            ve.tensor_scalar(m_nrm[:, i % 2, 0:NOPE], m_raw[:, i % 2, 0:NOPE], one, None, ALU.mult)
                            ve.tensor_scalar(m_nrm[:, i % 2, NOPE:QK], kpe_rot[:, i - LT, :], one, None, ALU.mult).then_inc(m_nrmd, 1)
                    elif kind == "mla_turn":
                        if i < LT:
                            cols = slice(i * P, (i + 1) * P)
                            ve.tensor_copy(m_qT[pp][:, cols], TR[:, 0:P])
                            ve.tensor_copy(m_q2T[pp][0:ROPE, cols], TR[0:ROPE, P:2 * P]).then_inc(tr_free, 1)
                        else:
                            cols = slice((i - LT) * P, (i - LT + 1) * P)
                            ve.tensor_scalar(m_kT[pp][:, cols], TR[:, 0:P], gk_nope[:, 0:1], None, ALU.mult)
                            ve.tensor_copy(m_k2T[pp][0:ROPE, cols], TR[0:ROPE, P:2 * P]).then_inc(tr_free, 1)
                    elif kind == "na_half" and i % 2:
                        tile = i // 2
                        lo = P if tile >= LT else 0
                        ve.wait_ge(pj_full, AT * g + tile + 1)
                        ve.tensor_copy(na_v[pp][:, tile, :], PJ[:, 2 * P - lo:3 * P - lo])
                        ve.tensor_copy(na_raw[:, tile % 2, lo:2 * P], PJ[:, 0:2 * P - lo]).then_inc(pj_free, 1)
                    elif kind == "na_norm":
                        ve.wait_ge(na_rsd, AT * g + i + 1)
                        c = 2 * (i % 2)
                        if i < LT:
                            ve.tensor_scalar(na_nrm[:, i % 2, 0:P], na_raw[:, i % 2, 0:P], n_rs[:, c:c + 1], None, ALU.mult)
                        ve.tensor_scalar(na_nrm[:, i % 2, P:2 * P], na_raw[:, i % 2, P:2 * P], n_rs[:, c + 1:c + 2],
                                         None, ALU.mult).then_inc(na_nrmd, 1)
                    elif kind == "na_turn":
                        cols = slice(i * P, (i + 1) * P)
                        if i < LT:
                            ve.tensor_scalar(na_qT[pp][:, cols], TR[:, 0:P], gqn[:, 0:1], None, ALU.mult)
                        ve.tensor_scalar(na_kT[pp][:, cols], TR[:, P:2 * P], gkn[:, 0:1], None, ALU.mult).then_inc(tr_free, 1)
                    elif kind == "mod":
                        if i % 4 == 0:
                            ve.wait_ge(brow_in, 16 * (2 * MODB + 2 * h + i // 4 + 1))
                            ve.tensor_tensor(modacc[:], MJ[:], brow[:], ALU.add).then_inc(mj_free, 1)
                        else:
                            ve.wait_ge(mj_free, small0 + place_in(plan, SMALL, ("mod", i - 1)) + 1)
                            ve.tensor_tensor(modacc[:], MJ[:], modacc[:], ALU.add).then_inc(mj_free, 1)
                    elif kind == "combine":
                        if some(16 * (2 * h + i)):
                            ve.wait_ge(modrow_out, 16 * (2 * h + i))
                        ve.tensor_copy(modrow[:], MJ[0:1, :]).then_inc(mj_free, 1)
                    elif kind == "scores":
                        tile = i // 2
                        ve.wait_ge(s_full, UNITS * h + i + 1)
                        if i % 2 == 0:
                            ve.tensor_reduce(mx[:, 0:1], S[:, 0:TOK], AX.X, ALU.max).then_inc(mx_part, 1)
                            ve.wait_ge(mx_part, MAXES * h + 3 * tile + 1)
                            ve.tensor_scalar(nmx, mx[:, 0:1], -1.0, None, ALU.mult).then_inc(mx_done, 1)
                        else:
                            ve.wait_ge(bias_in, 16 * (h + 1))
                            carry_wait(ve, 16 * (h + 1), passed)
                            lo = (ROWS - 2 - 2 * tile) * GRID_W
                            ve.tensor_tensor_reduce(biased[:, 0:SEQ], S[:, 0:SEQ], bias_h[:, lo:lo + SEQ], 1.0, NEG,
                                                    ALU.add, ALU.max, mx[:, 0:1]).then_inc(mx_part, 1)
                            ve.tensor_scalar(biased[:, SEQ:TOK], S[:, SEQ:TOK], 1.0, None, ALU.mult, ALU.max,
                                             accum_out=mx[:, 1:2]).then_inc(mx_part, 1)
                            ve.wait_ge(mx_part, MAXES * h + 3 * tile + 3)
                            ve.tensor_scalar(nmx, mx[:, 0:1], mx[:, 1:2], -1.0, ALU.max, ALU.mult).then_inc(mx_done, 1)
                    elif kind == "turn":
                        ve.wait_ge(t_full, UNITS * h + i + 1)
                        ve.reciprocal(rinv[:, i % 2:i % 2 + 1], lsum[:, i % 2:i % 2 + 1]).then_inc(rinv_done, 1)
                        ve.tensor_copy(probsT[:, 0:4, :], PT[:, 0:512].rearrange("p (a b) -> p a b", b=P)).then_inc(pt_a, 1)

            turn_of_head(-1, 1, True, False, first=True)
            turn_of_head(0, 0, True, True)
            with ve.Fori(0, (HEADS - 2) // 2) as two:
                turn_of_head(2 * two + 1, 1, True, True)
                turn_of_head(2 * two + 2, 0, True, True)
            turn_of_head(HEADS - 1, 1, False, True)

            for tile in range(LT):
                for q in range(4):
                    n = 4 * tile + q
                    bank = (TR, PT)[n % 2]
                    ve.wait_ge(dt_full, n + 1)
                    for i in range(4):
                        k = 4 * q + i
                        last = ve.tensor_scalar(mixT[:, k, tile * P:(tile + 1) * P], bank[:, i * P:(i + 1) * P],
                                                gout[:, k:k + 1], None, ALU.mult)
                    last.then_inc(dt_free, 1)
            ve.engine_nop().then_inc(y_free, 2)
            ve.wait_ge(xr_in, 16)
            ve.wait_ge(gate1_in, 16)
            with ve.Fori(0, MODB) as nb:
                for tile in range(LT):
                    ve.wait_ge(y_full, LT * nb + tile + 1)
                    bank = (PJ, MJ)[tile % 2]
                    ve.tensor_tensor(gated[:, tile % 2, :], bank[:], gate1_b[:, bass.ts(nb, NB)], ALU.mult).then_inc(y_free, 1)
                    ve.wait_ge(y_free, LT * nb + tile + 3)
                    ve.tensor_tensor(x1[:, tile, bass.ts(nb, NB)], x1[:, tile, bass.ts(nb, NB)], gated[:, tile % 2, :],
                                     ALU.add).then_inc(x1_done, 1)

            ve.wait_ge(mod2_in, 32)
            ve.wait_ge(g2_in, 16)
            ve.scalar_tensor_tensor(scale2_b[:], scale2_b[:], 1.0, h2[:, 1, :], ALU.add, ALU.mult).then_inc(mul2_set, 1)
            ve.wait_ge(mul2_set, 1)

            def copy_h2T(tile):
                for q in range(4):
                    n = 4 * tile + q
                    bank = (TR, PT)[n % 2]
                    ve.wait_ge(et_full, n + 1)
                    ve.tensor_copy(h2T[:, tile % 2, 4 * q:4 * q + 4, :], bank[:, 0:512].rearrange("p (a b) -> p a b", b=P)).then_inc(et_free, 1)

            def router(tile):
                p = probs_r[:, tile % 2, :]
                ve.wait_ge(lg_full, tile + 1)
                ve.tensor_reduce(mx[:, 0:1], O[:, 0:N_EXP], AX.X, ALU.max).then_inc(lg_mx, 1)
                ve.wait_ge(lg_mx, tile + 1)
                ve.tensor_scalar(nmx, mx[:, 0:1], -1.0, None, ALU.mult).then_inc(lg_nm, 1)
                ve.wait_ge(lg_exp, tile + 1)
                ve.reciprocal(rinv[:, 0:1], lsum[:, tile % 2:tile % 2 + 1]).then_inc(lg_rec, 1)
                ve.wait_ge(lg_rec, tile + 1)
                ve.tensor_scalar(p, p, rinv[:, 0:1], None, ALU.mult).then_inc(lg_aff, 1)

            def copy_aff(tile):
                ve.wait_ge(at_full, tile + 1)
                ve.tensor_copy(affT[0:N_EXP, tile * P:(tile + 1) * P], O[0:N_EXP, P:2 * P]).then_inc(at_free, 1)

            for tile in range(LT):
                ve.wait_ge(e_rsd, tile + 1)
                ve.scalar_tensor_tensor(h2[:, tile % 2, :], x1[:, tile, :], d_rs[:, tile:tile + 1], scale2_b[:],
                                        ALU.mult, ALU.mult).then_inc(e_mul, 1)
                ve.wait_ge(e_mul, tile + 1)
                ve.tensor_tensor(h2[:, tile % 2, :], h2[:, tile % 2, :], shift2_b[:], ALU.add).then_inc(h2_done, 1)
                copy_h2T(tile)
                if tile >= 1:
                    copy_aff(tile - 1)
                router(tile)
            copy_aff(LT - 1)

            ve.wait_ge(at_free, LT)
            scores_e = affT[0:N_EXP, :]
            for r in range(CAP // 8):
                eight = slice(8 * r, 8 * r + 8)
                if some(3 * r):
                    ve.wait_ge(top_step, 3 * r)
                ve.max(topv[:, eight], scores_e).then_inc(top_step, 1)
                ve.wait_ge(top_step, 3 * r + 1)
                ve.max_index(topi[:, eight], topv[:, eight], scores_e).then_inc(top_step, 1)
                ve.wait_ge(top_step, 3 * r + 2)
                ve.match_replace(scores_e, topv[:, eight], scores_e, -1.0).then_inc(top_step, 1)
            ve.tensor_copy(topf[:], topi[:]).then_inc(top_step, 1)
            ve.wait_ge(sp_full, 1)
            ve.tensor_copy(idx_e[:], O[0:CAP, 0:N_EXP]).then_inc(idx_done, 1)
            for half in range(2):
                rows = slice(64 * half, 64 * half + CAP)
                ve.tensor_copy(idx_pair[rows, :], O[rows, half:N_EXP:2]).then_inc(idx_done, 1)
                ve.tensor_copy(g_pair[rows, :], O[rows, 32 + half:32 + N_EXP:2]).then_inc(idx_done, 1)
            ve.wait_ge(idx_done, 5)

            def next_rows(pair):
                ve.tensor_copy(idx_now[:], idx_pair[:, bass.ds(pair, 1)]).then_inc(rows_set, 1)

            def copy_xsT(pair):
                for q in range(4):
                    ve.wait_ge(xt2_full, 4 * pair + q + 1)
                    bank = (TR, O)[q % 2]
                    ve.tensor_copy(xsT[:, 4 * q:4 * q + 4, :], bank[:].rearrange("p (a b) -> p a b", b=P)).then_inc(xt2_free, 1)

            def expert_pair(pair, last):
                if not last:
                    ve.wait_ge(xs_in, 16 * (pair + 1))
                    next_rows(pair + 1)
                for b in range(2):
                    ve.wait_ge(silu_done, 2 * pair + b + 1)
                    cols = slice(b * NB, (b + 1) * NB)
                    ve.tensor_tensor(act[:, cols], PT[:, cols], act[:, cols], ALU.mult).then_inc(act_done, 1)
                if not last:
                    copy_xsT(pair + 1)
                for q in range(2):
                    ve.wait_ge(at2_full, 2 * pair + q + 1)
                    ve.tensor_copy(actT[:, 4 * q:4 * q + 4, :], (PJ, MJ)[q][:].rearrange("p (a b) -> p a b", b=P)).then_inc(at2_free, 1)
                if some(32 * pair):
                    ve.wait_ge(sc_out, 32 * pair)
                ve.tensor_copy(idx_even[:], idx_e[:, bass.ds(2 * pair, 1)]).then_inc(pay_set, 1)
                ve.tensor_copy(idx_odd[:], idx_e[:, bass.ds(2 * pair + 1, 1)]).then_inc(pay_set, 1)
                ve.tensor_copy(g_now[:], g_pair[:, bass.ds(pair, 1)]).then_inc(pay_set, 1)
                ve.wait_ge(pay_set, 3 * (pair + 1))
                ve.wait_ge(moe_used, PIECES * (pair + 1))
                for b in range(4):
                    bank = (S, PT)[b // 2][:, (b % 2) * NB:(b % 2 + 1) * NB]
                    cols = slice(b * NB, (b + 1) * NB)
                    ve.scalar_tensor_tensor(y_sb[:, cols], bank, g_now[:, 0:1], gate2_b[:, cols], ALU.mult, ALU.mult).then_inc(y_done, 1)

            next_rows(0)
            copy_xsT(0)
            ve.wait_ge(gate2_in, 16)
            ve.wait_ge(x1_out, 16)
            expert_pair(0, False)
            with ve.Fori(1, PAIRS - 1) as pair:
                expert_pair(pair, False)
            expert_pair(PAIRS - 1, True)


INPUTS = ["tokens", "c", "c_ctx", "w_mod", "b_mod", "g_norm1", "w_in", "g_qa", "w_qb", "g_kva", "w_kvb", "g_q_mla",
          "g_k_mla", "g_q_na", "g_k_na", "rpb_na", "g_out_mla", "g_out_na", "w_out", "g_norm2", "w_router",
          "w_gate", "w_up", "w_down", "ident", "cos2", "sin2", "anti", "colmask", "sel"]


def shape_constants():
    tok = np.arange(SEQ)
    n_freq = ROPE // 4
    inv = np.float32(10000.0) ** (-np.arange(n_freq, dtype=np.float32) / np.float32(n_freq))
    row, col = (tok // GRID_W).astype(np.float32), (tok % GRID_W).astype(np.float32)
    ang = np.concatenate([row[:, None] * inv, col[:, None] * inv], axis=-1).astype(np.float32)
    cos, sin = np.cos(ang).astype(np.float32), np.sin(ang).astype(np.float32)

    def by_tile(a):
        return np.ascontiguousarray(a.reshape(LT, P, ROPE).transpose(1, 0, 2))

    o, m = np.arange(OFFS)[:, None], np.arange(2 * GRID_W - 1)[None]
    anti = (m == GRID_W - 1 + NA_KW - 1 - o).astype(np.float32)
    q = np.arange(P)[:, None] % GRID_W
    start = np.clip(q - NA_KW // 2, 0, GRID_W - NA_KW)
    key = np.arange(GRID_W)[None]
    inside = (key >= start) & (key < start + NA_KW)
    sel = (np.arange(P)[:, None] % 32 == np.arange(2)[None]).astype(np.float32)
    return {
        "ident": np.eye(P, dtype=np.float32),
        "cos2": by_tile(np.concatenate([cos, cos], axis=-1)),
        "sin2": by_tile(np.concatenate([-sin, sin], axis=-1)),
        "anti": anti,
        "colmask": np.where(inside, 0.0, -1e30).astype(np.float32),
        "sel": sel,
    }


def kernel(**inputs):
    import concourse.bacc as bacc
    from concourse.bass_utils import run_bass_kernel_spmd

    arrays = {k: np.ascontiguousarray(v) for k, v in inputs.items() if k not in ("x", "ctx")}
    arrays["tokens"] = np.concatenate([np.asarray(inputs["x"])[0], np.asarray(inputs["ctx"])[0]], axis=0)
    arrays |= shape_constants()
    arrays = {k: arrays[k] for k in INPUTS}
    nc = bacc.Bacc("TRN2", target_bir_lowering=False, num_devices=1)
    t = {k: nc.dram_tensor(f"in_{k}", a.shape, mybir.dt.from_np(a.dtype), kind="ExternalInput").ap() for k, a in arrays.items()}
    out = nc.dram_tensor("out_x", (1, SEQ, D), F32, kind="ExternalOutput").ap()
    build_layer(nc, t, out)
    r = run_bass_kernel_spmd(nc, [{f"in_{k}": a for k, a in arrays.items()}], core_ids=[0])
    return r.results[0]["out_x"]
```

```python
from contextlib import ExitStack

import numpy as np

import concourse.bass as bass
from concourse import mybir

F32 = mybir.dt.float32
F32R = mybir.dt.float32r
U32 = mybir.dt.uint32
ALU = mybir.AluOpType
ACT = mybir.ActivationFunctionType
AX = mybir.AxisListType

P = 128
D = 2048
KD = D // P
SEQ = 512
CTX = 256
TOK = SEQ + CTX
LT = SEQ // P
AT = TOK // P
GRID_W = 64
ROWS = SEQ // GRID_W
HEADS = 8
NOPE = 128
ROPE = 64
QK = NOPE + ROPE
VD = 128
Q_RANK = 512
KV_RANK = 256
NA_D = 128
NA_KH = 8
NA_KW = 16
IN_MLA = Q_RANK + KV_RANK + ROPE
NA_W = HEADS * NA_D
N_EXP = 16
F_EXP = 1024
CAP = 2 * SEQ // N_EXP
EPS = 1e-6
MLA_SCALE = QK ** -0.5
NA_SCALE = NA_D ** -0.5
NB = 512
MODB = D // NB
NEG = -3.0e38
OFFS = 2 * NA_KW - 1
DROWS = 2 * NA_KH - 1
BIAS_J = 2 * NA_KH - 2
BIAS_N = BIAS_J * GRID_W
UNITS = 2 * LT
PAIRS = N_EXP // 2
KF = F_EXP // P
RING = 8
PIECES = KD + KF
SLOT_AT = [0, 2, 1, 3, 5, 6, 4, 7]


def some(count):
    return not isinstance(count, int) or count > 0


def carry_wait(eng, count, passed):
    if not isinstance(count, int):
        eng.sem_inc(passed, 1)


def head_plan(prep, attend):
    plan = []
    for s in range(13):
        if attend and s == 9:
            plan.append(("combine", 0))
        if prep and s < LT + AT:
            plan.append(("mla_proj", s))
        if prep and 1 <= s <= LT + AT:
            plan.append(("mla_turn", s - 1))
        if prep and s < 2 * AT:
            plan.append(("na_half", s))
        if prep and s < LT + AT:
            plan.append(("mla_norm", s))
        if attend and s >= 5:
            plan.append(("mod", s - 5))
        if attend and 2 <= s < UNITS + 2:
            plan.append(("pv", s - 2))
        if attend and 1 <= s < UNITS + 1:
            plan.append(("turn", s - 1))
        if attend and s < UNITS:
            plan.append(("scores", s))
        if prep and s % 2 and s < 2 * AT:
            plan.append(("na_norm", s // 2))
        if prep and s % 2 == 0 and s >= 2:
            plan.append(("na_turn", s // 2 - 1))
    if attend:
        plan.append(("combine", 1))
    return plan


def place_in(plan, kinds, step):
    return [x for x in plan if x[0] in kinds].index(step)


SMALL = ("mla_proj", "mod", "combine")
TURNS = ("mla_turn", "na_turn")
PREP_SMALL = LT + AT
LOOP_SMALL = LT + AT + 8 + 2
HEAD_TURNS = LT + 2 * AT
MAXES = 3 * LT


class Arena:

    def __init__(self, tensor):
        self.tensor = tensor

    def take(self, at, *dims):
        n = int(np.prod(dims))
        flat = self.tensor[:, at:at + n]
        if len(dims) == 1:
            return flat
        names = "abc"[:len(dims)]
        sizes = dict(zip(names[1:], dims[1:]))
        return flat.rearrange(f"p ({' '.join(names)}) -> p {' '.join(names)}", **sizes)


def build_layer(nc, t, out):
    ctx = ExitStack()
    with ctx:
        def sb(name, shape, dt=F32):
            return ctx.enter_context(nc.sbuf_tensor(name, shape, dt))

        def ps(name, shape):
            return ctx.enter_context(nc.psum_tensor(name, shape, F32))

        def sem(name):
            return ctx.enter_context(nc.semaphore(name))

        def dram(name, shape):
            return nc.dram_tensor(name, shape, F32, kind="Internal").ap()

        bias_d = dram("bias_d", (HEADS, P, BIAS_N))
        modrow_d = dram("modrow_d", (4, D))
        o_d = dram("o_d", (SEQ, D))
        h2_d = dram("h2_d", (SEQ, D))

        K = 256
        arena = Arena(sb("arena", [P, 194 * K]))
        arena_at = nc.sbuf_base - 4 * 194 * K

        def own(name, at, *dims, dt=F32R):
            return nc.alloc_sbuf_tensor_at(name, [P, *dims], dt, offset=arena_at + 4 * at)[:]

        hT = arena.take(0, KD, TOK)
        slab = arena.take(48 * K, KD, 384)
        modw = [arena.take(a * K, 4, NB) for a in (72, 80, 48, 56)]
        cqT = arena.take(88 * K, Q_RANK // P, SEQ)
        ckvT = arena.take(96 * K, KV_RANK // P, TOK)
        kpe_rot = arena.take(102 * K, AT, ROPE)
        x_in = arena.take(104 * K, 2, D)
        xn = arena.take(120 * K, 2, D)
        bias_all = arena.take(161 * K, HEADS * BIAS_J, GRID_W)
        w_mla = arena.take(104 * K, KD, IN_MLA)
        raw_b = arena.take(182 * K, 2, IN_MLA)
        norm_b = arena.take(182 * K + 2 * IN_MLA, Q_RANK + KV_RANK)
        junk_b = arena.take(157 * K, IN_MLA)
        at = [104 * K]

        def head_buf(*dims):
            a = at[0]
            at[0] += int(np.prod(dims))
            return arena.take(a, *dims)

        na_qT = [head_buf(SEQ) for _ in range(2)]
        na_kT = [head_buf(TOK) for _ in range(2)]
        na_v = [head_buf(AT, NA_D) for _ in range(2)]
        m_qT = [head_buf(SEQ) for _ in range(2)]
        m_q2T = [head_buf(SEQ) for _ in range(2)]
        m_kT = [head_buf(TOK) for _ in range(2)]
        m_k2T = [head_buf(TOK) for _ in range(2)]
        m_v = [head_buf(AT, VD) for _ in range(2)]
        probs = head_buf(TOK)
        biased = head_buf(TOK)
        probsT = head_buf(AT, P)
        na_raw = head_buf(2, 256)
        na_nrm = head_buf(2, 256)
        m_raw = head_buf(2, 256)
        m_nrm = head_buf(2, QK)
        m_junk = head_buf(QK)
        na_junk = head_buf(2 * NA_D)
        o_sb = head_buf(UNITS, VD)
        wq = head_buf(Q_RANK // P, QK)
        wkv = head_buf(KV_RANK // P, NOPE + VD)
        bias_h = head_buf(BIAS_N)
        assert at[0] <= 182 * K
        w_raw = [own(f"w_raw{i}", 16 * i * K, KD // 2, NB, dt=F32) for i in range(2)]
        w_low = [own(f"w_low{i}", 16 * i * K, KD // 2, NB) for i in range(2)]
        w_high = [own(f"w_high{i}", (32 + 16 * i) * K, KD // 2, NB) for i in range(2)]
        o_in = [arena.take(a * K, D) for a in (112, 120, 160, 168)]
        h2T = arena.take(128 * K, KD, SEQ)
        mix_high = own("mix_high", 128 * K, KD, SEQ)
        mix_low = own("mix_low", 80 * K, KD, SEQ)
        x1 = arena.take(160 * K, LT, D)
        gate1_b = arena.take(64 * K, D)
        junk_d = arena.take(72 * K, 2, 1024)
        scale2_b = arena.take(112 * K, D)
        shift2_b = arena.take(72 * K, D)
        h2 = arena.take(120 * K, D)
        moe_w = [arena.take(16 * s * K, 4, F_EXP) for s in range(RING)]
        moe_wd = [arena.take(16 * s * K, 2, D) for s in range(RING)]
        xs = arena.take(128 * K, D)
        xsT = arena.take(136 * K, KD, P)
        gate2_b = arena.take(144 * K, D)
        act = arena.take(152 * K, F_EXP)
        actT = arena.take(156 * K, KF, P)
        y_sb = arena.take(164 * K, D)

        ident = sb("ident", [P, P])
        cos2 = sb("cos2", [P, LT, ROPE])
        sin2 = sb("sin2", [P, LT, ROPE])
        anti = arena.take(192 * K, 2 * GRID_W - 1)[0:OFFS]
        colmask = arena.take(192 * K + 128, GRID_W)
        sel = sb("sel", [P, 2])
        rpbT = arena.take(192 * K + 192, HEADS, DROWS)[0:OFFS]
        ccol = sb("ccol", [P, 2, KD])
        cexp = sb("cexp", [P, 2, KD])
        csil = sb("csil", [P, KD, 32])
        g1 = sb("g1", [P, KD])
        gqa = sb("gqa", [P, Q_RANK // P])
        gkva = sb("gkva", [P, KV_RANK // P])
        gq_b = sb("gq_b", [P, QK])
        gkt_b = sb("gkt_b", [P, ROPE])
        gk_nope = sb("gk_nope", [P, 1])
        gqn = sb("gqn", [P, 1])
        gkn = sb("gkn", [P, 1])
        gout = sb("gout", [P, KD])
        modcol = sb("modcol", [P, 2 * KD, 2])
        mul1 = sb("mul1", [P, KD, 2])
        halves = sb("halves", [P, 2])
        modacc = sb("modacc", [P, NB])
        brow = sb("brow", [P, NB])
        modrow = sb("modrow", [1, NB])
        gated = [modacc, brow]
        w_router = cos2[:].rearrange("p t (a e) -> p (t a) e", e=N_EXP)
        st = sb("st", [P, 64])
        rope_t = sb("rope_t", [P, 2, ROPE])
        kpe_eps = sb("kpe_eps", [P, AT])
        probs_r = sb("probs_r", [P, 2, N_EXP])
        affT = arena.take(192 * K, SEQ)
        topv = arena.take(155 * K, CAP)[0:N_EXP]
        topi = arena.take(155 * K + CAP, CAP)[0:N_EXP].bitcast(U32)
        topf = arena.take(155 * K + 2 * CAP, CAP)[0:N_EXP]
        idx_pair = sb("idx_pair", [P, PAIRS], U32)
        idx_e = sb("idx_e", [CAP, N_EXP], U32)
        g_pair = sb("g_pair", [P, PAIRS])
        idx_now = sb("idx_now", [P, 1], U32)
        idx_even = sb("idx_even", [CAP, 1], U32)
        idx_odd = sb("idx_odd", [CAP, 1], U32)
        g_now = sb("g_now", [P, 1])
        x_ss, x_ms, x_rstd = st[:, 0:2], st[:, 2:4], st[:, 4:6]
        b_ss, b_ms, b_rstd = (st[:, a:a + 6] for a in (6, 12, 18))
        m_ss, m_ms, m_rs = st[:, 24:26], st[:, 26:28], st[:, 28:30]
        n_ss, n_ms, n_rs = (st[:, a:a + 4] for a in (30, 34, 38))
        mx, nmx, lsum, rinv = st[:, 42:44], st[:, 44:45], st[:, 45:47], st[:, 47:49]
        d_ss, d_ms, d_rs = (st[:, a:a + 4] for a in (50, 54, 58))
        g_ss, g_ms, g_rs = (st[:, a:a + 2 * LT] for a in (0, 8, 16))

        S = ps("S", [P, 1024])
        PT = ps("PT", [P, 1024])
        PJ = ps("PJ", [P, 512])
        MJ = ps("MJ", [P, 512])
        TR = ps("TR", [P, 512])
        O = ps("O", [P, 512])

        c_in, first_in, const_in = sem("c_in"), sem("first_in"), sem("const_in")
        zeroed = sem("zeroed")
        half_set = sem("half_set")
        c_exp, c_rec, c_sil = sem("c_exp"), sem("c_rec"), sem("c_sil")
        bt_full, bt_free, bias_out = sem("bt_full"), sem("bt_free"), sem("bias_out")
        x_got = [sem("x_got0"), sem("x_got1")]
        x_ssd, x_msd, x_rsd, x_nrm = sem("x_ssd"), sem("x_msd"), sem("x_rsd"), sem("x_nrm")
        xt_full, xt_free = sem("xt_full"), sem("xt_free")
        mod_in = [sem(f"mod_in{i}") for i in range(4)]
        brow_in = sem("brow_in")
        ma_full, ma_used, ma_sum, ma_col, ma_free = (sem(n) for n in ("ma_full", "ma_used", "ma_sum", "ma_col", "ma_free"))
        mul_set, h_ready = sem("mul_set"), sem("h_ready")
        wm_in = [sem(f"wm_in{i}") for i in range(4)]
        b_full, b_free, b_ssd, b_msd, b_rsd, b_nrm = (sem(n) for n in ("b_full", "b_free", "b_ssd", "b_msd", "b_rsd", "b_nrm"))
        bt2_full, bt2_free, kpe_g, kpe_part, kpe_done, kpe_pre = (sem(n) for n in ("bt2_full", "bt2_free", "kpe_g", "kpe_part", "kpe_done", "kpe_pre"))
        slab_in = [sem(f"slab_in{i}") for i in range(4)]
        slab_used, mw_in, bias_in = sem("slab_used"), sem("mw_in"), sem("bias_in")
        pj_full, pj_free, na_ssd, na_msd, na_rsd, na_nrmd = (sem(n) for n in ("pj_full", "pj_free", "na_ssd", "na_msd", "na_rsd", "na_nrmd"))
        mj_full, mj_free, m_ssd, m_msd, m_rsd, m_nrmd, rope_part, m_rope = (
            sem(n) for n in ("mj_full", "mj_free", "m_ssd", "m_msd", "m_rsd", "m_nrmd", "rope_part", "m_rope"))
        tr_full, tr_free = sem("tr_full"), sem("tr_free")
        s_full, mx_part, mx_done, exp_done = sem("s_full"), sem("mx_part"), sem("mx_done"), sem("exp_done")
        t_full, pt_a, pt_b, rinv_done = sem("t_full"), sem("pt_a"), sem("pt_b"), sem("rinv_done")
        v_full, o_free, o_out, modrow_out = sem("v_full"), sem("o_free"), sem("o_out"), sem("modrow_out")
        wo_in = [sem("wo_in0"), sem("wo_in1")]
        high_done, low_done, first_half_used, mix_high_done, y_start = (
            sem(n) for n in ("high_done", "low_done", "first_half_used", "mix_high_done", "y_start"))
        o_got = [sem(f"o_got{i}") for i in range(LT)]
        xr_in, gate1_in = sem("xr_in"), sem("gate1_in")
        d_ssd, d_msd, d_rsd, d_nrm = sem("d_ssd"), sem("d_msd"), sem("d_rsd"), sem("d_nrm")
        dt_full, dt_free, y_full, y_free, x1_done = (sem(n) for n in ("dt_full", "dt_free", "y_full", "y_free", "x1_done"))
        mod2_in, g2_in, mul2_set = sem("mod2_in"), sem("g2_in"), sem("mul2_set")
        e_ssd, e_msd, e_rsd, e_mul, h2_done = sem("e_ssd"), sem("e_msd"), sem("e_rsd"), sem("e_mul"), sem("h2_done")
        h2_out = sem("h2_out")
        x1_out, router_in = sem("x1_out"), sem("router_in")
        et_full, et_free, lg_full, lg_mx, lg_nm, lg_exp, lg_rec, lg_aff, at_full, at_free = (
            sem(n) for n in ("et_full", "et_free", "lg_full", "lg_mx", "lg_nm", "lg_exp", "lg_rec", "lg_aff", "at_full", "at_free"))
        top_step, sp_full, idx_done = sem("top_step"), sem("sp_full"), sem("idx_done")
        moe_in = [sem(f"moe_in{i}") for i in range(RING)]
        moe_used = sem("moe_used")
        gate2_in, rows_set, pay_set, xs_in = sem("gate2_in"), sem("rows_set"), sem("pay_set"), sem("xs_in")
        xt2_full, xt2_free = sem("xt2_full"), sem("xt2_free")
        silu_done, act_done, at2_full, at2_free, y_done, sc_out = (
            sem(n) for n in ("silu_done", "act_done", "at2_full", "at2_free", "y_done", "sc_out"))

        w_in, w_mod, b_mod = t["w_in"][0], t["w_mod"][0], t["b_mod"]
        N_FIRST, N_CONST = 5, 12
        GROUPS = 4

        def mod_piece(block, kq):
            return w_mod[kq * 512:(kq + 1) * 512, bass.ts(block, NB)].rearrange("(k p) n -> p k n", p=P)

        def slab_cols(g, kq, which):
            return w_in[kq * 512:(kq + 1) * 512, bass.ds(IN_MLA + which * NA_W + g * NA_D, NA_D)].rearrange(
                "(k p) n -> p k n", p=P)

        def moe_piece(pair, i, up=0):
            if i < KD:
                w = t["w_up"][0] if up else t["w_gate"][0]
                return w[bass.ds(pair * 2, 2), i * P:(i + 1) * P, :].rearrange("e p n -> p e n")
            return t["w_down"][0][bass.ds(pair * 2, 2), (i - KD) * P:(i - KD + 1) * P, :].rearrange("e p n -> p e n")

        block = ctx.enter_context(nc.Block())

        passed = sem("passed")

        @block.sync
        def _(sp):
            for b in range(2):
                for kq in range(4):
                    if b:
                        sp.wait_ge(ma_used, 4 * (b - 1) + kq + 1)
                    sp.dma_start(modw[kq], mod_piece(b, kq)).then_inc(mod_in[kq], 16)
                if b == 0:
                    sp.wait_ge(zeroed, 2)
                else:
                    sp.wait_ge(ma_sum, b)
                sp.dma_start(brow[0:2, :], b_mod[:, b * NB:(b + 1) * NB].partition_broadcast(2)).then_inc(brow_in, 16)
            with sp.Fori(2, 2 * MODB) as b:
                for kq in range(4):
                    sp.wait_ge(ma_used, 4 * (b - 1) + kq + 1)
                    sp.dma_start(modw[kq], mod_piece(b, kq)).then_inc(mod_in[kq], 16)
                sp.wait_ge(ma_sum, b)
                sp.dma_start(brow[0:2, :], b_mod[:, bass.ts(b, NB)].partition_broadcast(2)).then_inc(brow_in, 16)
            sp.wait_ge(ma_sum, 2 * MODB)
            sp.dma_start(brow[0:1, :], b_mod[:, bass.ts(2 * MODB, NB)]).then_inc(brow_in, 16)
            sp.wait_ge(xt_full, 4 * AT)
            for kq in range(4):
                sp.dma_start(w_mla[:, 4 * kq:4 * kq + 4, :],
                             w_in[kq * 512:(kq + 1) * 512, 0:IN_MLA].rearrange("(k p) n -> p k n", p=P)).then_inc(wm_in[kq], 16)
            sp.wait_ge(bt_free, GRID_W // 4)
            sp.dma_start(bias_d.rearrange("h p n -> p h n"), bias_all.rearrange("p (h j) c -> p h (j c)", h=HEADS)).then_inc(bias_out, 16)

            sp.wait_ge(bias_out, 16)

            def loads(h, prep, attend, first=False):
                g = h + 1
                plan = head_plan(prep, attend)
                base = PREP_SMALL + LOOP_SMALL * h if not first else 0

                def small(step):
                    return base + place_in(plan, SMALL, step) + 1

                if prep:
                    if not first:
                        last = place_in(head_plan(True, not isinstance(h, int) or h > 0), SMALL, ("mla_proj", LT + AT - 1)) + 1
                        before = 0 if isinstance(h, int) and h == 0 else PREP_SMALL + LOOP_SMALL * (h - 1)
                        sp.wait_ge(mj_full, before + last)
                    sp.dma_start(wq[:], t["w_qb"][0][:, bass.ds(g * QK, QK)].rearrange("(k p) n -> p k n", p=P)).then_inc(mw_in, 16)
                    sp.dma_start(wkv[:], t["w_kvb"][0][:, bass.ds(g * (NOPE + VD), NOPE + VD)].rearrange("(k p) n -> p k n", p=P)).then_inc(mw_in, 16)
                    for kq in range(4):
                        if first:
                            sp.wait_ge(ma_used, 8 * MODB)
                        elif kq < 2:
                            sp.wait_ge(slab_used, h + 1)
                        else:
                            sp.wait_ge(pj_full, AT * (h + 1))
                        for which in range(3):
                            sp.dma_start(slab[:, 4 * kq:4 * kq + 4, which * NA_D:(which + 1) * NA_D],
                                         slab_cols(g, kq, which)).then_inc(slab_in[kq], 16)
                if first:
                    sp.dma_start(bias_h[:], bias_d[0]).then_inc(bias_in, 16)
                    return
                for i in range(8):
                    if i >= 2:
                        sp.wait_ge(mj_full, small(("mod", i - 2)))
                    elif isinstance(h, int) and h == 0:
                        sp.wait_ge(ma_used, 8 * MODB)
                    else:
                        sp.wait_ge(mj_full, PREP_SMALL + LOOP_SMALL * (h - 1)
                                 + place_in(head_plan(True, True), SMALL, ("mod", 6 + i)) + 1)
                    sp.dma_start(modw[i % 2], mod_piece(2 * MODB + 2 * h + i // 4, i % 4)).then_inc(mod_in[i % 2], 16)
                    if i == 4:
                        sp.wait_ge(mj_free, small(("mod", 0)))
                        sp.dma_start(brow[0:1, :], b_mod[:, bass.ts(2 * MODB + 2 * h + 1, NB)]).then_inc(brow_in, 16)
                    if i == 5 and prep:
                        sp.wait_ge(mx_done, UNITS * (h + 1))
                        sp.dma_start(bias_h[:], bias_d[bass.ds(h + 1, 1)].rearrange("a p n -> p (a n)")).then_inc(bias_in, 16)
                    if i == 7 and prep:
                        sp.wait_ge(mj_free, small(("mod", 4)))
                        sp.dma_start(brow[0:1, :], b_mod[:, bass.ts(2 * MODB + 2 * h + 2, NB)]).then_inc(brow_in, 16)

            loads(-1, True, False, first=True)
            loads(0, True, True)
            with sp.Fori(1, HEADS - 1) as h:
                loads(h, True, True)
            sp.wait_ge(pj_full, AT * HEADS)
            def load_w_out(piece):
                nb, half = piece // 2, piece % 2
                sp.dma_start(w_raw[half], t["w_out"][0][half * (D // 2):(half + 1) * (D // 2), nb * NB:(nb + 1) * NB].rearrange(
                    "(k p) n -> p k n", p=P)).then_inc(wo_in[half], 16)

            for piece in range(2):
                load_w_out(piece)
            loads(HEADS - 1, False, True)

            sp.wait_ge(o_out, 16 * UNITS * HEADS)
            for i in range(LT):
                sp.dma_start(o_in[i][:], o_d[i * P:(i + 1) * P, :]).then_inc(o_got[i], 16)
            sp.wait_ge(modrow_out, 16 * 2 * HEADS)
            sp.dma_start(gate1_b[:], modrow_d[0:1, :].partition_broadcast(P)).then_inc(gate1_in, 16)

            def moe_load(pair, i, n_slot):
                s = SLOT_AT[n_slot]
                if i < KD:
                    sp.dma_start(moe_w[s][:, 0:2, :], moe_piece(pair, i)).then_inc(moe_in[n_slot], 16)
                    sp.dma_start(moe_w[s][:, 2:4, :], moe_piece(pair, i, up=1)).then_inc(moe_in[n_slot], 16)
                else:
                    sp.dma_start(moe_wd[s], moe_piece(pair, i)).then_inc(moe_in[n_slot], 32)

            sp.wait_ge(dt_full, 4 * LT)
            sp.dma_start(x1[:], t["tokens"][0:SEQ, :].rearrange("(t p) n -> p t n", p=P)).then_inc(xr_in, 16)
            sp.dma_start(scale2_b[:], modrow_d[2:3, :].partition_broadcast(P)).then_inc(mod2_in, 16)
            sp.dma_start(shift2_b[:], modrow_d[1:2, :].partition_broadcast(P)).then_inc(mod2_in, 16)
            sp.dma_start(h2[:], t["g_norm2"].partition_broadcast(P)).then_inc(g2_in, 16)
            with nc.allow_non_contiguous_dma(reason="64-byte rows of the router"):
                sp.dma_start(w_router, t["w_router"][0].rearrange("(k p) e -> p k e", p=P)).then_inc(router_in, 16)
            for piece in range(2, 2 * MODB):
                if piece % 2 == 0:
                    sp.wait_ge(first_half_used, piece // 2)
                else:
                    sp.wait_ge(y_full, LT * (piece // 2))
                load_w_out(piece)
            sp.wait_ge(first_half_used, MODB)
            for n in range(2):
                moe_load(0, n, n)
            for i in range(LT):
                sp.wait_ge(x1_done, LT * (MODB - 1) + i + 1)
                sp.dma_start(out[0][i * P:(i + 1) * P, :], x1[:, i, :]).then_inc(x1_out, 16)
                if i == LT - 1:
                    for n in range(2, 4):
                        moe_load(0, n, n)
                sp.wait_ge(h2_done, i + 1)
                sp.dma_start(h2_d[i * P:(i + 1) * P, :], h2[:]).then_inc(h2_out, 16)
            for n in range(4, 7):
                moe_load(0, n, n)
            sp.wait_ge(lg_full, LT)
            sp.dma_start(gate2_b[:], modrow_d[3:4, :].partition_broadcast(P)).then_inc(gate2_in, 16)
            sp.wait_ge(h2_out, 16 * LT)
            moe_load(0, 7, 7)
            with sp.Fori(0, PAIRS - 1) as pair:
                for i in range(PIECES):
                    sp.wait_ge(moe_used, PIECES * pair + i + 1)
                    carry_wait(sp, PIECES * pair + i + 1, passed)
                    n = i + RING
                    if n < PIECES:
                        moe_load(pair, n, n % RING)
                    else:
                        moe_load(pair + 1, n - PIECES, n % RING)
            for i in range(PIECES - RING):
                sp.wait_ge(moe_used, PIECES * (PAIRS - 1) + i + 1)
                moe_load(PAIRS - 1, i + RING, i % RING)
            sp.wait_ge(sc_out, 32 * PAIRS)
            sp.wait_ge(x1_out, 16 * LT)

        @block.tensor
        def _(pe):
            def bias_columns(grp):
                if grp >= 2:
                    pe.wait_ge(bt_free, grp - 1)
                for i in range(4):
                    c = 4 * grp + i
                    for a in range(2):
                        mm = pe.matmul(S[64 * a:64 * a + 64, 512 * (grp % 2) + i * 112:512 * (grp % 2) + (i + 1) * 112].rearrange("p (h j) -> p h j", h=HEADS),
                                       anti[:, GRID_W - 1 - c:2 * GRID_W - 1 - c], rpbT[:, :, 1 - a:1 - a + BIAS_J],
                                       start=True, stop=True)
                mm.then_inc(bt_full, 1)

            def turn_rows(tile, par, first):
                pe.wait_ge(x_nrm, tile + 1)
                for q in range(4):
                    if not (first and q < 2):
                        pe.wait_ge(xt_free, 4 * tile + q - 1)
                    bank = (TR, O)[q % 2]
                    for i in range(4):
                        k = 4 * q + i
                        mm = pe.transpose(bank[:, i * P:(i + 1) * P], xn[:, par, k * P:(k + 1) * P], ident[:])
                    mm.then_inc(xt_full, 1)

            def mod_block(b):
                for kq in range(4):
                    pe.wait_ge(mod_in[kq], 16 * (b + 1))
                    for j in range(4):
                        mm = pe.matmul(PJ[32 * j:32 * j + 32, :], csil[:, 4 * kq + j, :], modw[kq][:, j, :],
                                       start=(kq == 0), stop=(kq == 3))
                    mm.then_inc(ma_used, 1)

            def mod_columns(b):
                pe.wait_ge(ma_sum, b + 1)
                for i in range(4):
                    mm = pe.matmul(MJ[:, 2 * i:2 * i + 2], modacc[:, i * P:(i + 1) * P], sel[:], start=True, stop=True)
                mm.then_inc(ma_col, 1)

            pe.wait_ge(c_sil, 1)
            for b in range(2 * MODB):
                mod_block(b)
                if b == 0:
                    pe.wait_ge(first_in, 16 * N_FIRST)
                for grp in range(GROUPS * b, min(GROUPS * (b + 1), GRID_W // 4)):
                    bias_columns(grp)
                mod_columns(b)
                if b < AT:
                    turn_rows(b, b % 2, b == 0)

            def turn_b(tile):
                pe.wait_ge(b_nrm, tile + 1)
                if some(tile):
                    pe.wait_ge(bt2_free, tile)
                if tile < LT:
                    for i in range(4):
                        pe.transpose(TR[:, i * P:(i + 1) * P], norm_b[:, i * P:(i + 1) * P], ident[:])
                for i in range(2):
                    mm = pe.transpose(O[:, i * P:(i + 1) * P], norm_b[:, Q_RANK + i * P:Q_RANK + (i + 1) * P], ident[:])
                mm.then_inc(bt2_full, 1)

            for tile in range(AT):
                bank = (S, PT)[tile % 2]
                if some(tile - 1):
                    pe.wait_ge(b_free, tile - 1)
                for k in range(KD):
                    if tile == 0:
                        pe.wait_ge(wm_in[k // 4], 16)
                        pe.wait_ge(h_ready, 2 * (k + 1))
                    lhs = hT[:, k, tile * P:(tile + 1) * P]
                    if tile < LT:
                        pe.matmul(bank[:, 0:Q_RANK], lhs, w_mla[:, k, 0:Q_RANK], start=(k == 0), stop=(k == KD - 1))
                    mm = pe.matmul(bank[:, 512:512 + IN_MLA - Q_RANK], lhs, w_mla[:, k, Q_RANK:IN_MLA],
                                   start=(k == 0), stop=(k == KD - 1))
                mm.then_inc(b_full, 1)
                if tile >= 1:
                    turn_b(tile - 1)
            turn_b(AT - 1)

            def turn_of_head(h, ap, prep, attend, first=False):
                g = h + 1
                pp = 1 - ap
                plan = head_plan(prep, attend)
                small0 = 0 if first else PREP_SMALL + LOOP_SMALL * h
                turn0 = HEAD_TURNS * g
                for step in plan:
                    kind, i = step
                    if kind in SMALL:
                        small = small0 + place_in(plan, SMALL, step)
                        if some(small):
                            pe.wait_ge(mj_free, small)
                    if kind in TURNS:
                        if some(turn0 + place_in(plan, TURNS, step)):
                            pe.wait_ge(tr_free, turn0 + place_in(plan, TURNS, step))
                    if kind == "mla_proj":
                        if i == 0:
                            pe.wait_ge(mw_in, 32 * (g + 1))
                            if first:
                                pe.wait_ge(bt2_free, AT)
                        if i < LT:
                            for k in range(Q_RANK // P):
                                mm = pe.matmul(MJ[:, 0:QK], cqT[:, k, i * P:(i + 1) * P], wq[:, k, :],
                                               start=(k == 0), stop=(k == Q_RANK // P - 1))
                        else:
                            for k in range(KV_RANK // P):
                                mm = pe.matmul(MJ[:, 0:NOPE + VD], ckvT[:, k, (i - LT) * P:(i - LT + 1) * P], wkv[:, k, :],
                                               start=(k == 0), stop=(k == KV_RANK // P - 1))
                        mm.then_inc(mj_full, 1)
                    elif kind == "mla_turn":
                        if i < LT:
                            pe.wait_ge(m_rope, LT * g + i + 1)
                        else:
                            pe.wait_ge(m_nrmd, (LT + AT) * g + i + 1)
                        pe.transpose(TR[:, 0:P], m_nrm[:, i % 2, 0:NOPE], ident[:])
                        pe.transpose(TR[0:ROPE, P:2 * P], m_nrm[:, i % 2, NOPE:QK], ident[:]).then_inc(tr_full, 1)
                    elif kind == "na_half":
                        tile, half = i // 2, i % 2
                        if half == 0:
                            if some(AT * g + tile):
                                pe.wait_ge(pj_free, AT * g + tile)
                        for k in range(8 * half, 8 * half + 8):
                            if tile == 0 and k % 4 == 0:
                                pe.wait_ge(slab_in[k // 4], 48 * (g + 1))
                            lo = 0 if tile < LT else NA_D
                            mm = pe.matmul(PJ[:, 0:3 * NA_D - lo], hT[:, k, tile * P:(tile + 1) * P], slab[:, k, lo:3 * NA_D],
                                           start=(k == 0), stop=(k == KD - 1))
                        if half:
                            mm.then_inc(pj_full, 1)
                        elif tile == AT - 1:
                            mm.then_inc(slab_used, 1)
                    elif kind == "mod":
                        pe.wait_ge(mod_in[i % 2], 16 * (2 * MODB + 4 * h + i // 2 + 1))
                        for j in range(4):
                            mm = pe.matmul(MJ[32 * j:32 * j + 32, :], csil[:, 4 * (i % 4) + j, :], modw[i % 2][:, j, :],
                                           start=True, stop=True)
                        mm.then_inc(mj_full, 1)
                    elif kind == "combine":
                        pe.matmul(MJ[0:2, :], sel[:], modacc[:], start=True, stop=True).then_inc(mj_full, 1)
                    elif kind == "scores":
                        tile = i // 2
                        if i == 0:
                            pe.wait_ge(tr_free, HEAD_TURNS * (h + 1))
                        cols = slice(tile * P, (tile + 1) * P)
                        for lo, n in ((0, SEQ), (SEQ, CTX)):
                            if i % 2 == 0:
                                pe.matmul(S[:, lo:lo + n], m_qT[ap][:, cols], m_kT[ap][:, lo:lo + n], start=True, stop=False)
                                mm = pe.matmul(S[:, lo:lo + n], m_q2T[ap][0:ROPE, cols], m_k2T[ap][0:ROPE, lo:lo + n],
                                               start=False, stop=True)
                            else:
                                mm = pe.matmul(S[:, lo:lo + n], na_qT[ap][:, cols], na_kT[ap][:, lo:lo + n], start=True, stop=True)
                        mm.then_inc(s_full, 1)
                    elif kind == "turn":
                        pe.wait_ge(exp_done, UNITS * h + i + 1)
                        for j in range(AT):
                            mm = pe.transpose(PT[:, j * P:(j + 1) * P], probs[:, j * P:(j + 1) * P], ident[:])
                        mm.then_inc(t_full, 1)
                    elif kind == "pv":
                        pe.wait_ge(pt_a, UNITS * h + i + 1)
                        pe.wait_ge(pt_b, UNITS * h + i + 1)
                        if some(UNITS * h + i):
                            pe.wait_ge(o_free, UNITS * h + i)
                        v = (m_v, na_v)[i % 2][ap]
                        for j in range(AT):
                            mm = pe.matmul(O[:, 0:VD], probsT[:, j, :], v[:, j, :], start=(j == 0), stop=(j == AT - 1))
                        mm.then_inc(v_full, 1)
                    elif kind == "na_turn":
                        pe.wait_ge(na_nrmd, AT * g + i + 1)
                        if i < LT:
                            pe.transpose(TR[:, 0:P], na_nrm[:, i % 2, 0:P], ident[:])
                        pe.transpose(TR[:, P:2 * P], na_nrm[:, i % 2, P:2 * P], ident[:]).then_inc(tr_full, 1)

            turn_of_head(-1, 1, True, False, first=True)
            turn_of_head(0, 0, True, True)
            with pe.Fori(0, (HEADS - 2) // 2) as two:
                turn_of_head(2 * two + 1, 1, True, True)
                turn_of_head(2 * two + 2, 0, True, True)
            turn_of_head(HEADS - 1, 1, False, True)

            def turn_out(tile):
                pe.wait_ge(d_nrm, tile + 1)
                for q in range(4):
                    n = 4 * tile + q
                    if some(n - 1):
                        pe.wait_ge(dt_free, n - 1)
                    bank = (TR, PT)[n % 2]
                    for i in range(4):
                        k = 4 * q + i
                        mm = pe.transpose(bank[:, i * P:(i + 1) * P], o_in[tile][:, k * P:(k + 1) * P], ident[:])
                    mm.then_inc(dt_full, 1)

            Y = [PJ[:], MJ[:], S[:, 0:NB], S[:, NB:2 * NB]]

            def project(piece, tile):
                half = piece % 2
                cols = slice(tile * P, (tile + 1) * P)
                for i in range(KD // 2):
                    k = half * (KD // 2) + i
                    pe.matmul(Y[tile], mix_high[:, k, cols], w_high[half][:, i, :], start=(k == 0), stop=False)
                    pe.matmul(Y[tile], mix_high[:, k, cols], w_low[half][:, i, :], start=False, stop=False)
                    mm = pe.matmul(Y[tile], mix_low[:, k, cols], w_high[half][:, i, :], start=False, stop=(k == KD - 1))
                return mm

            turn_out(0)
            pe.wait_ge(y_start, 1)
            for tile in range(LT):
                if tile + 1 < LT:
                    turn_out(tile + 1)
                pe.wait_ge(dt_free, 4 * (tile + 1))
                pe.wait_ge(low_done, 1)
                mm = project(0, tile)
            mm.then_inc(first_half_used, 1)
            for piece in range(1, 2 * MODB - 1):
                pe.wait_ge(low_done, piece + 1)
                for tile in range(LT):
                    if piece % 2:
                        project(piece, tile).then_inc(y_full, 1)
                    else:
                        pe.wait_ge(y_free, LT * (piece // 2 - 1) + tile + 1)
                        mm = project(piece, tile)
                if piece % 2 == 0:
                    mm.then_inc(first_half_used, 1)

            def router(tile):
                pe.wait_ge(et_free, 4 * (tile + 1))
                if some(tile):
                    pe.wait_ge(at_free, tile)
                pe.wait_ge(router_in, 16)
                for k in range(KD):
                    mm = pe.matmul(O[:, 0:N_EXP], h2T[:, k, tile * P:(tile + 1) * P], w_router[:, k, :], start=(k == 0), stop=(k == KD - 1))
                mm.then_inc(lg_full, 1)

            def turn_aff(tile):
                pe.wait_ge(lg_aff, tile + 1)
                pe.transpose(O[0:N_EXP, P:2 * P], probs_r[:, tile % 2, :], ident[:]).then_inc(at_full, 1)

            def turn_h2(tile):
                pe.wait_ge(h2_done, tile + 1)
                for q in range(4):
                    n = 4 * tile + q
                    if some(n - 1):
                        pe.wait_ge(et_free, n - 1)
                    bank = (TR, PT)[n % 2]
                    for i in range(4):
                        k = 4 * q + i
                        mm = pe.transpose(bank[:, i * P:(i + 1) * P], h2[:, k * P:(k + 1) * P], ident[:])
                    mm.then_inc(et_full, 1)
                if tile >= 1:
                    turn_aff(tile - 1)
                router(tile)

            pe.wait_ge(low_done, 2 * MODB)
            for tile in range(LT):
                project(2 * MODB - 1, tile).then_inc(y_full, 1)
                if tile >= 1:
                    turn_h2(tile - 1)
            turn_h2(LT - 1)
            turn_aff(LT - 1)
            pe.wait_ge(top_step, 3 * CAP // 8 + 1)
            for src, lo in ((topf, 0), (topv, 32)):
                for half in range(2):
                    mm = pe.matmul(O[64 * half:64 * half + CAP, lo:lo + N_EXP], src[:], ident[0:N_EXP, 0:N_EXP],
                                   start=True, stop=True)
            mm.then_inc(sp_full, 1)

            def turn_xs(pair):
                pe.wait_ge(xs_in, 16 * (pair + 1))
                for q in range(4):
                    if some(4 * pair + q - 1):
                        pe.wait_ge(xt2_free, 4 * pair + q - 1)
                    bank = (TR, O)[q % 2]
                    for i in range(4):
                        k = 4 * q + i
                        mm = pe.transpose(bank[:, i * P:(i + 1) * P], xs[:, k * P:(k + 1) * P], ident[:])
                    mm.then_inc(xt2_full, 1)

            GU = [S[:, 0:512], S[:, 512:1024], PT[:, 0:512], PT[:, 512:1024]]

            def expert_pair(pair, last):
                pe.wait_ge(xt2_free, 4 * (pair + 1))
                if some(4 * pair):
                    pe.wait_ge(y_done, 4 * pair)
                for k in range(KD):
                    pe.wait_ge(moe_in[k % RING], 32 * (3 * pair + k // RING + 1))
                    w = moe_w[SLOT_AT[k % RING]]
                    for b in range(4):
                        for e in range(2):
                            mm = pe.matmul(GU[b][64 * e:64 * e + CAP, :], xsT[:, k, 64 * e:64 * e + CAP],
                                           w[:, 2 * (b // 2) + e, (b % 2) * NB:(b % 2 + 1) * NB],
                                           start=(k == 0), stop=(k == KD - 1))
                    mm.then_inc(moe_used, 1)
                if not last:
                    turn_xs(pair + 1)
                pe.wait_ge(act_done, 2 * (pair + 1))
                for q in range(2):
                    if some(2 * pair + q):
                        pe.wait_ge(at2_free, 2 * pair + q)
                    for i in range(4):
                        f = 4 * q + i
                        mm = pe.transpose(PJ[:, i * P:(i + 1) * P] if q == 0 else MJ[:, i * P:(i + 1) * P],
                                          act[:, f * P:(f + 1) * P], ident[:])
                    mm.then_inc(at2_full, 1)
                pe.wait_ge(at2_free, 2 * pair + 2)
                for f in range(KF):
                    n = KD + f
                    pe.wait_ge(moe_in[n % RING], 32 * (3 * pair + n // RING + 1))
                    w = moe_wd[SLOT_AT[n % RING]]
                    for b in range(4):
                        for e in range(2):
                            mm = pe.matmul(GU[b][64 * e:64 * e + CAP, :], actT[:, f, 64 * e:64 * e + CAP],
                                           w[:, e, b * NB:(b + 1) * NB], start=(f == 0), stop=(f == KF - 1))
                    mm.then_inc(moe_used, 1)

            turn_xs(0)
            expert_pair(0, False)
            with pe.Fori(1, PAIRS - 1) as pair:
                expert_pair(pair, False)
            expert_pair(PAIRS - 1, True)

        @block.scalar
        def _(sc):
            with nc.allow_non_contiguous_dma(reason="small vectors onto the partitions"):
                sc.dma_start(ccol[:, 0, :], t["c"].rearrange("b (k p) -> p (b k)", p=P)).then_inc(c_in, 16)
                sc.dma_start(ccol[:, 1, :], t["c_ctx"].rearrange("(k p) -> p k", p=P)).then_inc(c_in, 16)
            sc.dma_start(sel[:], t["sel"]).then_inc(first_in, 16)
            sc.dma_start(ident[:], t["ident"]).then_inc(first_in, 16)
            sc.dma_start(anti[:], t["anti"]).then_inc(first_in, 16)
            sc.dma_start(colmask[:], t["colmask"]).then_inc(first_in, 16)
            with nc.allow_non_contiguous_dma(reason="small vectors onto the partitions"):
                sc.dma_start(rpbT[:], t["rpb_na"][0].rearrange("h r o -> o h r")).then_inc(first_in, 16)
            sc.wait_ge(c_in, 32)
            sc.activation(cexp[:], ccol[:], ACT.Exp, scale=-1.0).then_inc(c_exp, 1)
            with nc.allow_non_contiguous_dma(reason="small vectors onto the partitions"):
                for dst, name in ((g1, "g_norm1"), (gqa, "g_qa"), (gkva, "g_kva"), (gqn, "g_q_na"), (gkn, "g_k_na")):
                    sc.dma_start(dst[:], t[name].rearrange("l (k p) -> p (l k)", p=P)).then_inc(const_in, 16)
                sc.dma_start(gk_nope[:], t["g_k_mla"][:, 0:NOPE].rearrange("l (k p) -> p (l k)", p=P)).then_inc(const_in, 16)
                sc.dma_start(gout[:, 0:8], t["g_out_mla"].rearrange("l (k p) -> p (l k)", p=P)).then_inc(const_in, 16)
                sc.dma_start(gout[:, 8:16], t["g_out_na"].rearrange("l (k p) -> p (l k)", p=P)).then_inc(const_in, 16)
            sc.dma_start(gq_b[:], t["g_q_mla"].partition_broadcast(P)).then_inc(const_in, 16)
            sc.dma_start(gkt_b[:], t["g_k_mla"][:, NOPE:QK].partition_broadcast(P)).then_inc(const_in, 16)
            sc.dma_start(cos2[:], t["cos2"]).then_inc(const_in, 16)
            sc.dma_start(sin2[:], t["sin2"]).then_inc(const_in, 16)

            def norm_rows(tile, par, n_par):
                sc.wait_ge(x_got[par], 16 * (n_par + 1))
                if some(4 * (tile - 1)):
                    sc.wait_ge(xt_full, 4 * (tile - 1))
                sc.activation(xn[:, par, :], x_in[:, par, :], ACT.Square, accum_out=x_ss[:, par:par + 1]).then_inc(x_ssd, 1)
                sc.wait_ge(x_rsd, tile + 1)
                sc.wait_ge(x_ssd, tile + 1)
                sc.activation(xn[:, par, :], x_in[:, par, :], ACT.Copy, scale=x_rstd[:, par:par + 1]).then_inc(x_nrm, 1)

            for par in range(2):
                norm_rows(par, par, 0)
            with sc.Fori(1, AT // 2) as pair:
                for par in range(2):
                    norm_rows(2 * pair + par, par, pair)

            for tile in range(AT):
                sc.wait_ge(b_free, tile + 1)
                r = raw_b[:, tile % 2, :]
                if tile < LT:
                    sc.activation(junk_b[:, 0:Q_RANK], r[:, 0:Q_RANK], ACT.Square,
                                  accum_out=b_ss[:, tile % 2 * 3:tile % 2 * 3 + 1])
                sc.activation(junk_b[:, Q_RANK:Q_RANK + KV_RANK], r[:, Q_RANK:Q_RANK + KV_RANK], ACT.Square,
                              accum_out=b_ss[:, tile % 2 * 3 + 1:tile % 2 * 3 + 2])
                sc.activation(junk_b[:, Q_RANK + KV_RANK:IN_MLA], r[:, Q_RANK + KV_RANK:IN_MLA], ACT.Square,
                              accum_out=b_ss[:, tile % 2 * 3 + 2:tile % 2 * 3 + 3]).then_inc(b_ssd, 1)

            def turn_of_head(h, prep, attend, first=False):
                g = h + 1
                plan = head_plan(prep, attend)
                small0 = 0 if first else PREP_SMALL + LOOP_SMALL * h
                for step in plan:
                    kind, i = step
                    if kind == "mla_proj":
                        sc.wait_ge(mj_free, small0 + place_in(plan, SMALL, step) + 1)
                        if some((LT + AT) * g + i):
                            sc.wait_ge(m_ssd, (LT + AT) * g + i)
                        n = QK if i < LT else NOPE
                        sc.activation(m_junk[:, 0:n], m_raw[:, i % 2, 0:n], ACT.Square,
                                      accum_out=m_ss[:, i % 2:i % 2 + 1]).then_inc(m_ssd, 1)
                    elif kind == "na_half" and i % 2:
                        tile = i // 2
                        sc.wait_ge(pj_free, AT * g + tile + 1)
                        if some(AT * g + tile):
                            sc.wait_ge(na_ssd, AT * g + tile)
                        if tile < LT:
                            sc.activation(na_junk[:, 0:P], na_raw[:, tile % 2, 0:P], ACT.Square,
                                          accum_out=n_ss[:, 2 * (tile % 2):2 * (tile % 2) + 1])
                        sc.activation(na_junk[:, P:2 * P], na_raw[:, tile % 2, P:2 * P], ACT.Square,
                                      accum_out=n_ss[:, 2 * (tile % 2) + 1:2 * (tile % 2) + 2]).then_inc(na_ssd, 1)
                    elif kind == "scores":
                        sc.wait_ge(mx_done, UNITS * h + i + 1)
                        src = S[:, 0:TOK] if i % 2 == 0 else biased
                        sc.activation(probs[:], src, ACT.Exp, bias=nmx, accum_out=lsum[:, i % 2:i % 2 + 1]).then_inc(exp_done, 1)
                    elif kind == "turn":
                        sc.wait_ge(t_full, UNITS * h + i + 1)
                        sc.copy(probsT[:, 4:6, :], PT[:, 512:768].rearrange("p (a b) -> p a b", b=P)).then_inc(pt_b, 1)
                    elif kind == "pv":
                        sc.wait_ge(v_full, UNITS * h + i + 1)
                        sc.wait_ge(rinv_done, UNITS * h + i + 1)
                        if i == 0:
                            if some(16 * UNITS * h):
                                sc.wait_ge(o_out, 16 * UNITS * h)
                        sc.activation(o_sb[:, i, :], O[:, 0:VD], ACT.Copy, scale=rinv[:, i % 2:i % 2 + 1]).then_inc(o_free, 1)
                        sc.wait_ge(o_free, UNITS * h + i + 1)
                        tile, group = i // 2, i % 2
                        sc.dma_start(o_d[tile * P:(tile + 1) * P, bass.ds(group * HEADS * VD + h * VD, VD)],
                                     o_sb[:, i, :]).then_inc(o_out, 16)
                    elif kind == "combine":
                        sc.wait_ge(mj_free, small0 + place_in(plan, SMALL, step) + 1)
                        sc.dma_start(modrow_d.rearrange("a (b n) -> (a b) n", n=NB)[bass.ds(2 * h + i, 1), :],
                                     modrow[:]).then_inc(modrow_out, 16)

            turn_of_head(-1, True, False, first=True)
            turn_of_head(0, True, True)
            with sc.Fori(1, HEADS - 1) as h:
                turn_of_head(h, True, True)
            turn_of_head(HEADS - 1, False, True)

            def high(piece):
                sc.wait_ge(wo_in[piece % 2], 16 * (piece // 2 + 1))
                if piece >= 2 and piece % 2 == 0:
                    sc.wait_ge(first_half_used, piece // 2)
                elif piece >= 2:
                    sc.wait_ge(y_full, LT * (piece // 2))
                sc.activation(w_high[piece % 2], w_raw[piece % 2], ACT.Copy).then_inc(high_done, 1)

            def square_out(tile):
                sc.wait_ge(o_got[tile], 16)
                if tile:
                    sc.wait_ge(d_ssd, tile)
                for half in range(2):
                    last = sc.activation(junk_d[:, half, :], o_in[tile][:, half * 1024:(half + 1) * 1024], ACT.Square,
                                         accum_out=g_ss[:, 2 * tile + half:2 * tile + half + 1])
                last.then_inc(d_ssd, 1)

            def high_mix(tile):
                for q in range(4):
                    n = 4 * tile + q
                    bank = (TR, PT)[n % 2]
                    sc.wait_ge(dt_full, n + 1)
                    for i in range(4):
                        k = 4 * q + i
                        last = sc.activation(mix_high[:, k, tile * P:(tile + 1) * P], bank[:, i * P:(i + 1) * P],
                                             ACT.Copy, scale=gout[:, k:k + 1])
                    last.then_inc(mix_high_done, 1)

            high(0)
            square_out(0)
            for tile in range(LT):
                if tile + 1 < LT:
                    square_out(tile + 1)
                high_mix(tile)
            for piece in range(1, 2 * MODB):
                high(piece)

            def router_exp(tile):
                sc.wait_ge(lg_nm, tile + 1)
                sc.activation(probs_r[:, tile % 2, :], O[:, 0:N_EXP], ACT.Exp, bias=nmx,
                              accum_out=lsum[:, tile % 2:tile % 2 + 1]).then_inc(lg_exp, 1)

            def square(tile):
                sc.wait_ge(x1_done, LT * (MODB - 1) + tile + 1)
                if tile == 0:
                    sc.wait_ge(mul2_set, 1)
                else:
                    sc.wait_ge(h2_out, 16 * tile)
                    sc.wait_ge(et_full, 4 * tile)
                sc.activation(h2[:], x1[:, tile, :], ACT.Square, accum_out=d_ss[:, tile:tile + 1]).then_inc(e_ssd, 1)

            square(0)
            square(1)
            for tile in range(LT):
                router_exp(tile)
                if tile + 2 < LT:
                    square(tile + 2)

            def expert_pair(pair):
                sc.wait_ge(moe_used, PIECES * pair + KD)
                if some(2 * pair):
                    sc.wait_ge(at2_full, 2 * pair)
                for b in range(2):
                    sc.activation(act[:, b * NB:(b + 1) * NB], S[:, b * NB:(b + 1) * NB], ACT.Silu).then_inc(silu_done, 1)

            expert_pair(0)
            with sc.Fori(1, PAIRS) as pair:
                expert_pair(pair)

        @block.gpsimd
        def _(po):
            po.memset(csil[:], 0.0).then_inc(zeroed, 1)
            po.memset(brow[:], 0.0).then_inc(zeroed, 1)
            po.memset(halves[:], -0.5).then_inc(half_set, 1)
            for par in range(2):
                po.dma_start(x_in[:, par, :], t["tokens"][par * P:(par + 1) * P, :]).then_inc(x_got[par], 16)
            po.wait_ge(half_set, 1)

            def root(ms, out_ap, done, n=1):
                po.tensor_tensor(out_ap, ms, halves[:, 0:n], ALU.pow).then_inc(done, 1)

            def row_rstd(tile, par):
                po.wait_ge(x_ssd, tile + 1)
                carry_wait(po, tile + 1, passed)
                po.tensor_scalar(x_ms[:, par:par + 1], x_ss[:, par:par + 1], 1.0 / D, EPS, ALU.mult, ALU.add).then_inc(x_msd, 1)
                po.wait_ge(x_msd, tile + 1)
                root(x_ms[:, par:par + 1], x_rstd[:, par:par + 1], x_rsd)

            for par in range(2):
                row_rstd(par, par)
            with po.Fori(1, AT // 2) as pair:
                tile = 2 * pair
                for par in range(2):
                    po.wait_ge(x_nrm, tile + par - 1)
                    carry_wait(po, tile + par - 1, passed)
                    po.dma_start(x_in[:, par, :], t["tokens"][bass.ds((tile + par) * P, P), :]).then_inc(x_got[par], 16)
                for par in range(2):
                    row_rstd(tile + par, par)

            def rotate(dst, rows, tile, scratch, done, n0):
                half = ROPE // 2
                po.tensor_tensor(scratch[:, 0, :], rows, cos2[:, tile, :], ALU.mult).then_inc(done, 1)
                po.tensor_tensor(scratch[:, 1, 0:half], rows[:, half:ROPE], sin2[:, tile, 0:half], ALU.mult).then_inc(done, 1)
                po.tensor_tensor(scratch[:, 1, half:ROPE], rows[:, 0:half], sin2[:, tile, half:ROPE], ALU.mult).then_inc(done, 1)
                po.wait_ge(done, n0 + 3)
                return po.tensor_tensor(dst, scratch[:, 0, :], scratch[:, 1, :], ALU.add)

            for tile in range(AT):
                p3 = tile % 2 * 3
                po.wait_ge(b_ssd, tile + 1)
                if tile < LT:
                    po.tensor_scalar(b_ms[:, p3:p3 + 1], b_ss[:, p3:p3 + 1], 1.0 / Q_RANK, EPS, ALU.mult, ALU.add)
                po.tensor_scalar(kpe_eps[:, tile:tile + 1], b_ss[:, p3 + 2:p3 + 3], 1.0 / QK, EPS, ALU.mult, ALU.add).then_inc(kpe_pre, 1)
                po.tensor_scalar(b_ms[:, p3 + 1:p3 + 2], b_ss[:, p3 + 1:p3 + 2], 1.0 / KV_RANK, EPS, ALU.mult, ALU.add).then_inc(b_msd, 1)
                po.wait_ge(b_msd, tile + 1)
                if tile < LT:
                    root(b_ms[:, p3:p3 + 2], b_rstd[:, p3:p3 + 2], b_rsd, 2)
                else:
                    root(b_ms[:, p3 + 1:p3 + 2], b_rstd[:, p3 + 1:p3 + 2], b_rsd)
                if tile < LT:
                    po.wait_ge(kpe_g, tile + 1)
                    rotate(kpe_rot[:, tile, :], kpe_rot[:, tile, :], tile, rope_t, kpe_part, 3 * tile).then_inc(kpe_done, 1)
                    po.wait_ge(kpe_done, tile + 1)

            def turn_of_head(h, prep, attend):
                g = h + 1
                for kind, i in head_plan(prep, attend):
                    if kind == "mla_proj":
                        n = (LT + AT) * g + i + 1
                        one = slice(i % 2, i % 2 + 1)
                        po.wait_ge(m_ssd, n)
                        carry_wait(po, n, passed)
                        if i < LT:
                            po.tensor_scalar(m_ms[:, one], m_ss[:, one], 1.0 / QK, EPS, ALU.mult, ALU.add).then_inc(m_msd, 1)
                        else:
                            po.tensor_scalar(m_ms[:, one], m_ss[:, one], 1.0 / QK, kpe_eps[:, i - LT:i - LT + 1],
                                             ALU.mult, ALU.add).then_inc(m_msd, 1)
                        po.wait_ge(m_msd, n)
                        root(m_ms[:, one], m_rs[:, one], m_rsd)
                    elif kind == "mla_norm" and i < LT:
                        po.wait_ge(m_nrmd, (LT + AT) * g + i + 1)
                        carry_wait(po, (LT + AT) * g + i + 1, passed)
                        tail = m_nrm[:, i % 2, NOPE:QK]
                        rotate(tail, tail, i, rope_t, rope_part, 3 * (LT * g + i)).then_inc(m_rope, 1)
                        po.wait_ge(m_rope, LT * g + i + 1)
                        carry_wait(po, LT * g + i + 1, passed)
                    elif kind == "na_half" and i % 2:
                        tile = i // 2
                        two = slice(2 * (tile % 2), 2 * (tile % 2) + 2) if tile < LT else slice(2 * (tile % 2) + 1, 2 * (tile % 2) + 2)
                        po.wait_ge(na_ssd, AT * g + tile + 1)
                        carry_wait(po, AT * g + tile + 1, passed)
                        po.tensor_scalar(n_ms[:, two], n_ss[:, two], 1.0 / NA_D, EPS, ALU.mult, ALU.add).then_inc(na_msd, 1)
                        po.wait_ge(na_msd, AT * g + tile + 1)
                        root(n_ms[:, two], n_rs[:, two], na_rsd, 2 if tile < LT else 1)

            turn_of_head(-1, True, False)
            turn_of_head(0, True, True)
            with po.Fori(1, HEADS - 1) as h:
                turn_of_head(h, True, True)

            for tile in range(LT):
                two = slice(2 * tile, 2 * tile + 2)
                po.wait_ge(d_ssd, tile + 1)
                po.tensor_scalar(g_ms[:, two], g_ss[:, two], 1.0 / (HEADS * VD), EPS, ALU.mult, ALU.add).then_inc(d_msd, 1)
                po.wait_ge(d_msd, tile + 1)
                root(g_ms[:, two], g_rs[:, two], d_rsd, 2)
            for tile in range(LT):
                one = slice(tile, tile + 1)
                po.wait_ge(e_ssd, tile + 1)
                po.tensor_scalar(d_ms[:, one], d_ss[:, one], 1.0 / D, EPS, ALU.mult, ALU.add).then_inc(e_msd, 1)
                po.wait_ge(e_msd, tile + 1)
                root(d_ms[:, one], d_rs[:, one], e_rsd)

            def gather(pair):
                po.wait_ge(rows_set, pair + 1)
                carry_wait(po, pair + 1, passed)
                po.indirect_dma_start(xs[:], None, h2_d, bass.IndirectOffsetOnAxis(ap=idx_now[:, 0:1], axis=0)).then_inc(xs_in, 16)

            def scatter(pair):
                po.wait_ge(pay_set, 3 * (pair + 1))
                carry_wait(po, 3 * (pair + 1), passed)
                po.wait_ge(y_done, 4 * (pair + 1))
                carry_wait(po, 4 * (pair + 1), passed)
                po.indirect_dma_start(out[0], bass.IndirectOffsetOnAxis(ap=idx_even[:, 0:1], axis=0), y_sb[0:CAP, :], None,
                                      compute_op=ALU.add).then_inc(sc_out, 16)
                po.wait_ge(sc_out, 32 * pair + 16)
                carry_wait(po, 32 * pair + 16, passed)
                po.indirect_dma_start(out[0], bass.IndirectOffsetOnAxis(ap=idx_odd[:, 0:1], axis=0), y_sb[64:64 + CAP, :], None,
                                      compute_op=ALU.add).then_inc(sc_out, 16)
                po.wait_ge(sc_out, 32 * pair + 32)
                carry_wait(po, 32 * pair + 32, passed)

            po.wait_ge(h2_out, 16 * LT)
            po.wait_ge(x1_out, 16 * LT)
            gather(0)

            def expert_pair(pair, last):
                if not last:
                    po.wait_ge(xt2_full, 4 * (pair + 1))
                    carry_wait(po, 4 * (pair + 1), passed)
                    gather(pair + 1)
                scatter(pair)

            expert_pair(0, False)
            with po.Fori(1, PAIRS - 1) as pair:
                expert_pair(pair, False)
            expert_pair(PAIRS - 1, True)

        @block.vector
        def _(ve):
            ve.wait_ge(c_exp, 1)
            ve.tensor_scalar(cexp[:], cexp[:], 1.0, None, ALU.add).then_inc(c_rec, 1)
            ve.wait_ge(c_rec, 1)
            ve.reciprocal(cexp[:], cexp[:]).then_inc(c_rec, 1)
            ve.wait_ge(c_rec, 2)
            ve.wait_ge(zeroed, 2)
            ve.tensor_tensor(csil[:, :, 0:2].rearrange("p k c -> p c k"), ccol[:], cexp[:], ALU.mult).then_inc(c_sil, 1)

            def mask_columns(grp):
                ve.wait_ge(bt_full, grp + 1)
                cols = slice(4 * grp, 4 * grp + 4)
                ve.tensor_tensor(bias_all[:, :, cols].rearrange("p r c -> p c r"),
                                 S[:, 512 * (grp % 2):512 * (grp % 2) + 448].rearrange("p (c r) -> p c r", c=4),
                                 colmask[:, cols].unsqueeze(2).broadcast_to([P, 4, HEADS * BIAS_J]), ALU.add).then_inc(bt_free, 1)

            def copy_turned(tile):
                for q in range(4):
                    ve.wait_ge(xt_full, 4 * tile + q + 1)
                    bank = (TR, O)[q % 2]
                    ve.tensor_copy(hT[:, 4 * q:4 * q + 4, tile * P:(tile + 1) * P],
                                   bank[:].rearrange("p (a b) -> p a b", b=P)).then_inc(xt_free, 1)

            ve.wait_ge(first_in, 16 * N_FIRST)
            for b in range(2 * MODB):
                ve.wait_ge(ma_used, 4 * b + 4)
                ve.wait_ge(brow_in, 16 * (b + 1))
                ve.tensor_tensor(modacc[:], PJ[:], brow[:], ALU.add).then_inc(ma_sum, 1)
                for grp in range(GROUPS * b, min(GROUPS * (b + 1), GRID_W // 4)):
                    mask_columns(grp)
                ve.wait_ge(ma_col, b + 1)
                ve.tensor_copy(modcol[:, 4 * b:4 * b + 4, :], MJ[:, 0:8].rearrange("p (a b) -> p a b", b=2)).then_inc(ma_free, 1)
                if b < AT:
                    copy_turned(b)
            ve.wait_ge(const_in, 16 * N_CONST)
            ve.wait_ge(ma_free, 2 * MODB)
            ve.scalar_tensor_tensor(mul1[:], modcol[:, KD:2 * KD, :], 1.0, g1[:].unsqueeze(2).broadcast_to([P, KD, 2]),
                                    ALU.add, ALU.mult).then_inc(mul_set, 1)
            ve.wait_ge(mul_set, 1)
            ve.wait_ge(xt_free, 4 * AT)
            for k in range(KD):
                for c, (lo, hi) in enumerate(((0, SEQ), (SEQ, TOK))):
                    ve.tensor_scalar(hT[:, k, lo:hi], hT[:, k, lo:hi], mul1[:, k, c:c + 1], modcol[:, k, c:c + 1],
                                     ALU.mult, ALU.add).then_inc(h_ready, 1)

            def copy_b(tile):
                ve.wait_ge(bt2_full, tile + 1)
                cols = slice(tile * P, (tile + 1) * P)
                if tile < LT:
                    for i in range(4):
                        ve.tensor_scalar(cqT[:, i, cols], TR[:, i * P:(i + 1) * P], gqa[:, i:i + 1], None, ALU.mult)
                for i in range(2):
                    last = ve.tensor_scalar(ckvT[:, i, cols], O[:, i * P:(i + 1) * P], gkva[:, i:i + 1], None, ALU.mult)
                last.then_inc(bt2_free, 1)

            for tile in range(AT):
                ve.wait_ge(b_full, tile + 1)
                bank = (S, PT)[tile % 2]
                r = raw_b[:, tile % 2, :]
                if tile == 0:
                    ve.wait_ge(bias_out, 16)
                if tile < LT:
                    ve.tensor_copy(r[:, 0:Q_RANK], bank[:, 0:Q_RANK])
                ve.tensor_copy(r[:, Q_RANK:IN_MLA], bank[:, 512:512 + IN_MLA - Q_RANK]).then_inc(b_free, 1)
                if tile >= 1:
                    copy_b(tile - 1)
                ve.wait_ge(b_free, tile + 1)
                ve.tensor_tensor(kpe_rot[:, tile, :], r[:, Q_RANK + KV_RANK:IN_MLA], gkt_b[:], ALU.mult).then_inc(kpe_g, 1)
                ve.wait_ge(b_rsd, tile + 1)
                p3 = tile % 2 * 3
                if tile < LT:
                    ve.tensor_scalar(norm_b[:, 0:Q_RANK], r[:, 0:Q_RANK], b_rstd[:, p3:p3 + 1], None, ALU.mult)
                ve.tensor_scalar(norm_b[:, Q_RANK:Q_RANK + KV_RANK], r[:, Q_RANK:Q_RANK + KV_RANK], b_rstd[:, p3 + 1:p3 + 2],
                                 None, ALU.mult).then_inc(b_nrm, 1)
            copy_b(AT - 1)
            ve.tensor_scalar(gq_b[:], gq_b[:], MLA_SCALE, None, ALU.mult).then_inc(mul_set, 1)
            ve.tensor_scalar(gqn[:], gqn[:], NA_SCALE, None, ALU.mult).then_inc(mul_set, 1)
            ve.wait_ge(mul_set, 3)
            ve.wait_ge(kpe_done, LT)

            def turn_of_head(h, ap, prep, attend, first=False):
                g = h + 1
                pp = 1 - ap
                plan = head_plan(prep, attend)
                small0 = 0 if first else PREP_SMALL + LOOP_SMALL * h
                turn0 = HEAD_TURNS * g
                for step in plan:
                    kind, i = step
                    if kind in SMALL:
                        small = small0 + place_in(plan, SMALL, step)
                        ve.wait_ge(mj_full, small + 1)
                    if kind in TURNS:
                        ve.wait_ge(tr_full, turn0 + place_in(plan, TURNS, step) + 1)
                    if kind == "mla_proj":
                        if i < LT:
                            ve.tensor_copy(m_raw[:, i % 2, 0:QK], MJ[:, 0:QK]).then_inc(mj_free, 1)
                        else:
                            ve.tensor_copy(m_v[pp][:, i - LT, :], MJ[:, NOPE:NOPE + VD])
                            ve.tensor_copy(m_raw[:, i % 2, 0:NOPE], MJ[:, 0:NOPE]).then_inc(mj_free, 1)
                    elif kind == "mla_norm":
                        ve.wait_ge(m_rsd, (LT + AT) * g + i + 1)
                        one = m_rs[:, i % 2:i % 2 + 1]
                        if i < LT:
                            ve.scalar_tensor_tensor(m_nrm[:, i % 2, :], m_raw[:, i % 2, 0:QK], one, gq_b[:],
                                                    ALU.mult, ALU.mult).then_inc(m_nrmd, 1)
                        else:
                            ve.tensor_scalar(m_nrm[:, i % 2, 0:NOPE], m_raw[:, i % 2, 0:NOPE], one, None, ALU.mult)
                            ve.tensor_scalar(m_nrm[:, i % 2, NOPE:QK], kpe_rot[:, i - LT, :], one, None, ALU.mult).then_inc(m_nrmd, 1)
                    elif kind == "mla_turn":
                        if i < LT:
                            cols = slice(i * P, (i + 1) * P)
                            ve.tensor_copy(m_qT[pp][:, cols], TR[:, 0:P])
                            ve.tensor_copy(m_q2T[pp][0:ROPE, cols], TR[0:ROPE, P:2 * P]).then_inc(tr_free, 1)
                        else:
                            cols = slice((i - LT) * P, (i - LT + 1) * P)
                            ve.tensor_scalar(m_kT[pp][:, cols], TR[:, 0:P], gk_nope[:, 0:1], None, ALU.mult)
                            ve.tensor_copy(m_k2T[pp][0:ROPE, cols], TR[0:ROPE, P:2 * P]).then_inc(tr_free, 1)
                    elif kind == "na_half" and i % 2:
                        tile = i // 2
                        lo = P if tile >= LT else 0
                        ve.wait_ge(pj_full, AT * g + tile + 1)
                        ve.tensor_copy(na_v[pp][:, tile, :], PJ[:, 2 * P - lo:3 * P - lo])
                        ve.tensor_copy(na_raw[:, tile % 2, lo:2 * P], PJ[:, 0:2 * P - lo]).then_inc(pj_free, 1)
                    elif kind == "na_norm":
                        ve.wait_ge(na_rsd, AT * g + i + 1)
                        c = 2 * (i % 2)
                        if i < LT:
                            ve.tensor_scalar(na_nrm[:, i % 2, 0:P], na_raw[:, i % 2, 0:P], n_rs[:, c:c + 1], None, ALU.mult)
                        ve.tensor_scalar(na_nrm[:, i % 2, P:2 * P], na_raw[:, i % 2, P:2 * P], n_rs[:, c + 1:c + 2],
                                         None, ALU.mult).then_inc(na_nrmd, 1)
                    elif kind == "na_turn":
                        cols = slice(i * P, (i + 1) * P)
                        if i < LT:
                            ve.tensor_scalar(na_qT[pp][:, cols], TR[:, 0:P], gqn[:, 0:1], None, ALU.mult)
                        ve.tensor_scalar(na_kT[pp][:, cols], TR[:, P:2 * P], gkn[:, 0:1], None, ALU.mult).then_inc(tr_free, 1)
                    elif kind == "mod":
                        if i % 4 == 0:
                            ve.wait_ge(brow_in, 16 * (2 * MODB + 2 * h + i // 4 + 1))
                            ve.tensor_tensor(modacc[:], MJ[:], brow[:], ALU.add).then_inc(mj_free, 1)
                        else:
                            ve.wait_ge(mj_free, small0 + place_in(plan, SMALL, ("mod", i - 1)) + 1)
                            ve.tensor_tensor(modacc[:], MJ[:], modacc[:], ALU.add).then_inc(mj_free, 1)
                    elif kind == "combine":
                        if some(16 * (2 * h + i)):
                            ve.wait_ge(modrow_out, 16 * (2 * h + i))
                        ve.tensor_copy(modrow[:], MJ[0:1, :]).then_inc(mj_free, 1)
                    elif kind == "scores":
                        tile = i // 2
                        ve.wait_ge(s_full, UNITS * h + i + 1)
                        if i % 2 == 0:
                            ve.tensor_reduce(mx[:, 0:1], S[:, 0:TOK], AX.X, ALU.max).then_inc(mx_part, 1)
                            ve.wait_ge(mx_part, MAXES * h + 3 * tile + 1)
                            ve.tensor_scalar(nmx, mx[:, 0:1], -1.0, None, ALU.mult).then_inc(mx_done, 1)
                        else:
                            ve.wait_ge(bias_in, 16 * (h + 1))
                            carry_wait(ve, 16 * (h + 1), passed)
                            lo = (ROWS - 2 - 2 * tile) * GRID_W
                            ve.tensor_tensor_reduce(biased[:, 0:SEQ], S[:, 0:SEQ], bias_h[:, lo:lo + SEQ], 1.0, NEG,
                                                    ALU.add, ALU.max, mx[:, 0:1]).then_inc(mx_part, 1)
                            ve.tensor_scalar(biased[:, SEQ:TOK], S[:, SEQ:TOK], 1.0, None, ALU.mult, ALU.max,
                                             accum_out=mx[:, 1:2]).then_inc(mx_part, 1)
                            ve.wait_ge(mx_part, MAXES * h + 3 * tile + 3)
                            ve.tensor_scalar(nmx, mx[:, 0:1], mx[:, 1:2], -1.0, ALU.max, ALU.mult).then_inc(mx_done, 1)
                    elif kind == "turn":
                        ve.wait_ge(t_full, UNITS * h + i + 1)
                        ve.reciprocal(rinv[:, i % 2:i % 2 + 1], lsum[:, i % 2:i % 2 + 1]).then_inc(rinv_done, 1)
                        ve.tensor_copy(probsT[:, 0:4, :], PT[:, 0:512].rearrange("p (a b) -> p a b", b=P)).then_inc(pt_a, 1)

            turn_of_head(-1, 1, True, False, first=True)
            turn_of_head(0, 0, True, True)
            with ve.Fori(0, (HEADS - 2) // 2) as two:
                turn_of_head(2 * two + 1, 1, True, True)
                turn_of_head(2 * two + 2, 0, True, True)
            turn_of_head(HEADS - 1, 1, False, True)

            def low(piece):
                ve.wait_ge(high_done, piece + 1)
                ve.tensor_tensor(w_low[piece % 2], w_raw[piece % 2], w_high[piece % 2].bitcast(F32), ALU.subtract).then_inc(low_done, 1)

            def scale_out(tile):
                ve.wait_ge(d_rsd, tile + 1)
                for half in range(2):
                    rows = o_in[tile][:, half * 1024:(half + 1) * 1024]
                    last = ve.tensor_scalar(rows, rows, g_rs[:, 2 * tile + half:2 * tile + half + 1], None, ALU.mult)
                last.then_inc(d_nrm, 1)

            ve.engine_nop().then_inc(y_start, 1)
            low(0)
            scale_out(0)
            for tile in range(LT):
                if tile + 1 < LT:
                    scale_out(tile + 1)
                for q in range(4):
                    n = 4 * tile + q
                    bank = (TR, PT)[n % 2]
                    ve.wait_ge(dt_full, n + 1)
                    ve.wait_ge(mix_high_done, n + 1)
                    for i in range(4):
                        k = 4 * q + i
                        cols = slice(tile * P, (tile + 1) * P)
                        last = ve.scalar_tensor_tensor(mix_low[:, k, cols], bank[:, i * P:(i + 1) * P], gout[:, k:k + 1],
                                                       mix_high[:, k, cols].bitcast(F32), ALU.mult, ALU.subtract)
                    last.then_inc(dt_free, 1)
            low(1)
            ve.wait_ge(xr_in, 16)
            ve.wait_ge(gate1_in, 16)

            def residual(nb, tile):
                ve.wait_ge(y_full, LT * nb + tile + 1)
                bank = (PJ[:], MJ[:], S[:, 0:NB], S[:, NB:2 * NB])[tile]
                cols = slice(nb * NB, (nb + 1) * NB)
                ve.tensor_tensor(gated[tile % 2][:], bank, gate1_b[:, cols], ALU.mult).then_inc(y_free, 1)
                ve.wait_ge(y_free, LT * nb + tile + 1)
                ve.tensor_tensor(x1[:, tile, cols], x1[:, tile, cols], gated[tile % 2][:], ALU.add).then_inc(x1_done, 1)

            for nb in range(MODB - 1):
                low(2 * nb + 2)
                for tile in range(LT):
                    residual(nb, tile)
                low(2 * nb + 3)

            ve.wait_ge(mod2_in, 32)
            ve.wait_ge(g2_in, 16)
            ve.scalar_tensor_tensor(scale2_b[:], scale2_b[:], 1.0, h2[:], ALU.add, ALU.mult).then_inc(mul2_set, 1)
            ve.wait_ge(mul2_set, 1)

            def modulate(tile):
                ve.wait_ge(e_rsd, tile + 1)
                ve.scalar_tensor_tensor(h2[:], x1[:, tile, :], d_rs[:, tile:tile + 1], scale2_b[:],
                                        ALU.mult, ALU.mult).then_inc(e_mul, 1)
                ve.wait_ge(e_mul, tile + 1)
                ve.tensor_tensor(h2[:], h2[:], shift2_b[:], ALU.add).then_inc(h2_done, 1)

            def copy_h2T(tile):
                for q in range(4):
                    n = 4 * tile + q
                    bank = (TR, PT)[n % 2]
                    ve.wait_ge(et_full, n + 1)
                    ve.tensor_copy(h2T[:, 4 * q:4 * q + 4, tile * P:(tile + 1) * P], bank[:, 0:512].rearrange("p (a b) -> p a b", b=P)).then_inc(et_free, 1)

            def router(tile):
                p = probs_r[:, tile % 2, :]
                ve.wait_ge(lg_full, tile + 1)
                ve.tensor_reduce(mx[:, 0:1], O[:, 0:N_EXP], AX.X, ALU.max).then_inc(lg_mx, 1)
                ve.wait_ge(lg_mx, tile + 1)
                ve.tensor_scalar(nmx, mx[:, 0:1], -1.0, None, ALU.mult).then_inc(lg_nm, 1)
                ve.wait_ge(lg_exp, tile + 1)
                ve.reciprocal(rinv[:, 0:1], lsum[:, tile % 2:tile % 2 + 1]).then_inc(lg_rec, 1)
                ve.wait_ge(lg_rec, tile + 1)
                ve.tensor_scalar(p, p, rinv[:, 0:1], None, ALU.mult).then_inc(lg_aff, 1)

            def copy_aff(tile):
                ve.wait_ge(at_full, tile + 1)
                ve.tensor_copy(affT[0:N_EXP, tile * P:(tile + 1) * P], O[0:N_EXP, P:2 * P]).then_inc(at_free, 1)

            for tile in range(LT):
                residual(MODB - 1, tile)
                if tile >= 1:
                    copy_h2T(tile - 1)
                if tile >= 2:
                    copy_aff(tile - 2)
                modulate(tile)
                if tile >= 1:
                    router(tile - 1)
            copy_h2T(LT - 1)
            copy_aff(LT - 2)
            router(LT - 1)
            copy_aff(LT - 1)

            ve.wait_ge(at_free, LT)
            scores_e = affT[0:N_EXP, :]
            for r in range(CAP // 8):
                eight = slice(8 * r, 8 * r + 8)
                if some(3 * r):
                    ve.wait_ge(top_step, 3 * r)
                ve.max(topv[:, eight], scores_e).then_inc(top_step, 1)
                ve.wait_ge(top_step, 3 * r + 1)
                ve.max_index(topi[:, eight], topv[:, eight], scores_e).then_inc(top_step, 1)
                ve.wait_ge(top_step, 3 * r + 2)
                ve.match_replace(scores_e, topv[:, eight], scores_e, -1.0).then_inc(top_step, 1)
            ve.tensor_copy(topf[:], topi[:]).then_inc(top_step, 1)
            ve.wait_ge(sp_full, 1)
            ve.tensor_copy(idx_e[:], O[0:CAP, 0:N_EXP]).then_inc(idx_done, 1)
            for half in range(2):
                rows = slice(64 * half, 64 * half + CAP)
                ve.tensor_copy(idx_pair[rows, :], O[rows, half:N_EXP:2]).then_inc(idx_done, 1)
                ve.tensor_copy(g_pair[rows, :], O[rows, 32 + half:32 + N_EXP:2]).then_inc(idx_done, 1)
            ve.wait_ge(idx_done, 5)

            def next_rows(pair):
                ve.tensor_copy(idx_now[:], idx_pair[:, bass.ds(pair, 1)]).then_inc(rows_set, 1)

            def copy_xsT(pair):
                for q in range(4):
                    ve.wait_ge(xt2_full, 4 * pair + q + 1)
                    bank = (TR, O)[q % 2]
                    ve.tensor_copy(xsT[:, 4 * q:4 * q + 4, :], bank[:].rearrange("p (a b) -> p a b", b=P)).then_inc(xt2_free, 1)

            def expert_pair(pair, last):
                if not last:
                    ve.wait_ge(xs_in, 16 * (pair + 1))
                    next_rows(pair + 1)
                for b in range(2):
                    ve.wait_ge(silu_done, 2 * pair + b + 1)
                    cols = slice(b * NB, (b + 1) * NB)
                    ve.tensor_tensor(act[:, cols], PT[:, cols], act[:, cols], ALU.mult).then_inc(act_done, 1)
                if not last:
                    copy_xsT(pair + 1)
                for q in range(2):
                    ve.wait_ge(at2_full, 2 * pair + q + 1)
                    ve.tensor_copy(actT[:, 4 * q:4 * q + 4, :], (PJ, MJ)[q][:].rearrange("p (a b) -> p a b", b=P)).then_inc(at2_free, 1)
                if some(32 * pair):
                    ve.wait_ge(sc_out, 32 * pair)
                ve.tensor_copy(idx_even[:], idx_e[:, bass.ds(2 * pair, 1)]).then_inc(pay_set, 1)
                ve.tensor_copy(idx_odd[:], idx_e[:, bass.ds(2 * pair + 1, 1)]).then_inc(pay_set, 1)
                ve.tensor_copy(g_now[:], g_pair[:, bass.ds(pair, 1)]).then_inc(pay_set, 1)
                ve.wait_ge(pay_set, 3 * (pair + 1))
                ve.wait_ge(moe_used, PIECES * (pair + 1))
                for b in range(4):
                    bank = (S, PT)[b // 2][:, (b % 2) * NB:(b % 2 + 1) * NB]
                    cols = slice(b * NB, (b + 1) * NB)
                    ve.scalar_tensor_tensor(y_sb[:, cols], bank, g_now[:, 0:1], gate2_b[:, cols], ALU.mult, ALU.mult).then_inc(y_done, 1)

            next_rows(0)
            copy_xsT(0)
            ve.wait_ge(gate2_in, 16)
            ve.wait_ge(x1_out, 16 * LT)
            expert_pair(0, False)
            with ve.Fori(1, PAIRS - 1) as pair:
                expert_pair(pair, False)
            expert_pair(PAIRS - 1, True)


INPUTS = ["tokens", "c", "c_ctx", "w_mod", "b_mod", "g_norm1", "w_in", "g_qa", "w_qb", "g_kva", "w_kvb", "g_q_mla",
          "g_k_mla", "g_q_na", "g_k_na", "rpb_na", "g_out_mla", "g_out_na", "w_out", "g_norm2", "w_router",
          "w_gate", "w_up", "w_down", "ident", "cos2", "sin2", "anti", "colmask", "sel"]


def shape_constants():
    tok = np.arange(SEQ)
    n_freq = ROPE // 4
    inv = np.float32(10000.0) ** (-np.arange(n_freq, dtype=np.float32) / np.float32(n_freq))
    row, col = (tok // GRID_W).astype(np.float32), (tok % GRID_W).astype(np.float32)
    ang = np.concatenate([row[:, None] * inv, col[:, None] * inv], axis=-1).astype(np.float32)
    cos, sin = np.cos(ang).astype(np.float32), np.sin(ang).astype(np.float32)

    def by_tile(a):
        return np.ascontiguousarray(a.reshape(LT, P, ROPE).transpose(1, 0, 2))

    o, m = np.arange(OFFS)[:, None], np.arange(2 * GRID_W - 1)[None]
    anti = (m == GRID_W - 1 + NA_KW - 1 - o).astype(np.float32)
    q = np.arange(P)[:, None] % GRID_W
    start = np.clip(q - NA_KW // 2, 0, GRID_W - NA_KW)
    key = np.arange(GRID_W)[None]
    inside = (key >= start) & (key < start + NA_KW)
    sel = (np.arange(P)[:, None] % 32 == np.arange(2)[None]).astype(np.float32)
    return {
        "ident": np.eye(P, dtype=np.float32),
        "cos2": by_tile(np.concatenate([cos, cos], axis=-1)),
        "sin2": by_tile(np.concatenate([-sin, sin], axis=-1)),
        "anti": anti,
        "colmask": np.where(inside, 0.0, -1e30).astype(np.float32),
        "sel": sel,
    }


def kernel(**inputs):
    import concourse.bacc as bacc
    from concourse.bass_utils import run_bass_kernel_spmd

    arrays = {k: np.ascontiguousarray(v) for k, v in inputs.items() if k not in ("x", "ctx")}
    arrays["tokens"] = np.concatenate([np.asarray(inputs["x"])[0], np.asarray(inputs["ctx"])[0]], axis=0)
    arrays |= shape_constants()
    arrays = {k: arrays[k] for k in INPUTS}
    nc = bacc.Bacc("TRN2", target_bir_lowering=False, num_devices=1)
    t = {k: nc.dram_tensor(f"in_{k}", a.shape, mybir.dt.from_np(a.dtype), kind="ExternalInput").ap() for k, a in arrays.items()}
    out = nc.dram_tensor("out_x", (1, SEQ, D), F32, kind="ExternalOutput").ap()
    build_layer(nc, t, out)
    r = run_bass_kernel_spmd(nc, [{f"in_{k}": a for k, a in arrays.items()}], core_ids=[0])
    return r.results[0]["out_x"]
```
